# Optimizing a Trainium2 kernel written in Bass

```python
import math
import jax, jax.numpy as jnp
from jax import lax
import numpy as np

D_MODEL = 2048
BATCH = 1
SEQ = 256
DEPTH = 1

HEAD_DIM = 128
N_HEADS = D_MODEL // HEAD_DIM
H_A = N_HEADS // 2
H_B = N_HEADS - H_A
D_A = H_A * HEAD_DIM
D_B = H_B * HEAD_DIM
D_PROJ = 3 * D_A + 3 * D_B + H_B
DILATED_PATTERNS = ((128, 1), (512, 4), (2048, 16))
NUM_BUCKETS = 32
MAX_DISTANCE = 2048
FOX_BLOCK = 128
D_FF = ((8 * D_MODEL // 3 + 127) // 128) * 128
RMS_EPS = 1e-6
NEG_INF = -1e30
ATTN_SCALE = HEAD_DIM ** -0.5

kernel_name = "hybrid_dilated_fox_macaron"

def rmsnorm(x, g):
    xf = x.astype(jnp.float32)
    y = xf * lax.rsqrt(jnp.mean(xf * xf, axis=-1, keepdims=True) + RMS_EPS)
    return (y * g.astype(jnp.float32)).astype(x.dtype)

def swiglu_ffn(x, w_in, w_out):
    gate, up = jnp.split(x @ w_in, 2, axis=-1)
    return (jax.nn.silu(gate) * up) @ w_out

def t5_causal_bucket(dist):
    max_exact = NUM_BUCKETS // 2
    d = dist.astype(jnp.float32)
    large = max_exact + (jnp.log(jnp.maximum(d, 1.0) / max_exact)
                         / math.log(MAX_DISTANCE / max_exact)
                         * (NUM_BUCKETS - max_exact)).astype(jnp.int32)
    large = jnp.minimum(large, NUM_BUCKETS - 1)
    return jnp.where(dist < max_exact, dist, large)

def dilated_window_partial(q, k, v, rel_table, window, dilation):
    B, S, H, D = q.shape
    m = window // dilation
    L = m
    span = dilation * L
    Sp = -(-S // span) * span
    n = Sp // dilation
    nb = n // L

    def to_sub(t):
        t = jnp.pad(t, ((0, 0), (0, Sp - S), (0, 0), (0, 0)))
        t = t.reshape(B, n, dilation, H, D).transpose(0, 2, 3, 1, 4)
        return t.reshape(B, dilation, H, nb, L, D)

    def with_prev(t):
        prev = jnp.pad(t, ((0, 0), (0, 0), (0, 0), (1, 0), (0, 0), (0, 0)))[:, :, :, :-1]
        return jnp.concatenate([prev, t], axis=4)

    qs = to_sub(q)
    kw = with_prev(to_sub(k))
    vw = with_prev(to_sub(v))

    iq = jnp.arange(L)[:, None] + L
    ik = jnp.arange(2 * L)[None, :]
    delta = iq - ik
    band = (delta >= 0) & (delta <= m)
    bucket = t5_causal_bucket(jnp.clip(delta, 0, None) * dilation)
    bias = rel_table[bucket].astype(jnp.float32).transpose(2, 0, 1)
    blk = jnp.arange(nb)
    key_ok = (blk[:, None] * L + ik - L) >= 0
    mask = band[None] & key_ok[:, None, :]

    logits = jnp.einsum('bzhnqd,bzhnkd->bzhnqk', qs, kw) * ATTN_SCALE + bias[:, None]
    logits = jnp.where(mask, logits, NEG_INF)
    mx = jnp.max(logits, axis=-1)
    p = jnp.exp(logits - mx[..., None])
    den = jnp.sum(p, axis=-1)
    num = jnp.einsum('bzhnqk,bzhnkd->bzhnqd', p, vw)

    def from_sub(t):
        rest = t.shape[5:]
        t = t.reshape((B, dilation, H, n) + rest)
        t = jnp.moveaxis(t, 3, 1)
        return t.reshape((B, Sp, H) + rest)[:, :S]

    return from_sub(num), from_sub(den), from_sub(mx)

def dilated_attention(q, k, v, rel_table):
    parts = [dilated_window_partial(q, k, v, rel_table, w, d) for (w, d) in DILATED_PATTERNS]
    mx = jnp.max(jnp.stack([pt[2] for pt in parts], axis=0), axis=0)
    num = None
    den = None
    for pnum, pden, pmx in parts:
        scale = jnp.exp(pmx - mx)
        num = pnum * scale[..., None] if num is None else num + pnum * scale[..., None]
        den = pden * scale if den is None else den + pden * scale
    return num / den[..., None]

def forgetting_attention(q, k, v, log_f):
    B, S, H, D = q.shape
    c = jnp.cumsum(log_f, axis=1)
    c_k = c.transpose(0, 2, 1)
    nblk = S // FOX_BLOCK
    q_blocks = q.reshape(B, nblk, FOX_BLOCK, H, D).transpose(1, 0, 3, 2, 4)
    c_blocks = c.reshape(B, nblk, FOX_BLOCK, H).transpose(1, 0, 3, 2)
    kpos = jnp.arange(S)

    def block(args):
        q_blk, c_blk, i = args
        qpos = i * FOX_BLOCK + jnp.arange(FOX_BLOCK)
        logits = (jnp.einsum('bhqd,bkhd->bhqk', q_blk, k) * ATTN_SCALE
                  + c_blk[..., None] - c_k[:, :, None, :])
        logits = jnp.where(kpos[None, :] <= qpos[:, None], logits, NEG_INF)
        p = jax.nn.softmax(logits, axis=-1)
        return jnp.einsum('bhqk,bkhd->bhqd', p, v)

    out = lax.map(block, (q_blocks, c_blocks, jnp.arange(nblk)))
    return out.transpose(1, 0, 3, 2, 4).reshape(B, S, H, D)

def setup_inputs(seed: int = 0) -> dict:
    key = jax.random.key(seed)
    ks = jax.random.split(key, 17)
    f32 = jnp.float32

    def gain(k, shape):
        return (1.0 + 0.02 * jax.random.normal(k, shape)).astype(f32)

    x = jax.random.normal(ks[0], (BATCH, SEQ, D_MODEL), f32)
    ffn1_norm = gain(ks[1], (DEPTH, D_MODEL))
    ffn1_w_in = jax.random.normal(ks[2], (DEPTH, D_MODEL, 2 * D_FF), f32) * D_MODEL ** -0.5
    ffn1_w_out = jax.random.normal(ks[3], (DEPTH, D_FF, D_MODEL), f32) * D_FF ** -0.5
    mix_norm = gain(ks[4], (DEPTH, D_MODEL))
    w_in = jax.random.normal(ks[5], (DEPTH, D_MODEL, D_PROJ), f32) * D_MODEL ** -0.5
    q_norm_a = gain(ks[6], (DEPTH, HEAD_DIM))
    k_norm_a = gain(ks[7], (DEPTH, HEAD_DIM))
    q_norm_b = gain(ks[8], (DEPTH, HEAD_DIM))
    k_norm_b = gain(ks[9], (DEPTH, HEAD_DIM))
    forget_bias = (jnp.linspace(1.0, 4.0, H_B, dtype=f32)[None, :]
                   + 0.1 * jax.random.normal(ks[10], (DEPTH, H_B), f32))
    rel_bias_table = 0.5 * jax.random.normal(ks[11], (NUM_BUCKETS, H_A), f32)
    w_out = jax.random.normal(ks[12], (DEPTH, D_A + D_B, D_MODEL), f32) * (D_A + D_B) ** -0.5
    ffn2_norm = gain(ks[13], (DEPTH, D_MODEL))
    ffn2_w_in = jax.random.normal(ks[14], (DEPTH, D_MODEL, 2 * D_FF), f32) * D_MODEL ** -0.5
    ffn2_w_out = jax.random.normal(ks[15], (DEPTH, D_FF, D_MODEL), f32) * D_FF ** -0.5
    return {"x": x, "ffn1_norm": ffn1_norm, "ffn1_w_in": ffn1_w_in, "ffn1_w_out": ffn1_w_out,
            "mix_norm": mix_norm, "w_in": w_in, "q_norm_a": q_norm_a, "k_norm_a": k_norm_a,
            "q_norm_b": q_norm_b, "k_norm_b": k_norm_b, "forget_bias": forget_bias,
            "rel_bias_table": rel_bias_table, "w_out": w_out, "ffn2_norm": ffn2_norm,
            "ffn2_w_in": ffn2_w_in, "ffn2_w_out": ffn2_w_out}

def reference(x, ffn1_norm, ffn1_w_in, ffn1_w_out, mix_norm, w_in, q_norm_a, k_norm_a,
              q_norm_b, k_norm_b, forget_bias, rel_bias_table, w_out, ffn2_norm,
              ffn2_w_in, ffn2_w_out):
    B, S, _ = x.shape
    splits = np.cumsum([D_A, D_A, D_A, D_B, D_B, D_B]).tolist()
    for l in range(DEPTH):
        x = x + 0.5 * swiglu_ffn(rmsnorm(x, ffn1_norm[l]), ffn1_w_in[l], ffn1_w_out[l])

        h = rmsnorm(x, mix_norm[l])
        proj = h @ w_in[l]
        qa, ka, va, qb, kb, vb, f_pre = jnp.split(proj, splits, axis=-1)

        def heads(t, n_h):
            return t.reshape(B, S, n_h, HEAD_DIM).astype(jnp.float32)

        qa = rmsnorm(heads(qa, H_A), q_norm_a[l])
        ka = rmsnorm(heads(ka, H_A), k_norm_a[l])
        va = heads(va, H_A)
        qb = rmsnorm(heads(qb, H_B), q_norm_b[l])
        kb = rmsnorm(heads(kb, H_B), k_norm_b[l])
        vb = heads(vb, H_B)
        log_f = jax.nn.log_sigmoid(f_pre.astype(jnp.float32) + forget_bias[l].astype(jnp.float32))

        out_a = dilated_attention(qa, ka, va, rel_bias_table)
        out_b = forgetting_attention(qb, kb, vb, log_f)
        mixed = jnp.concatenate([out_a.reshape(B, S, D_A), out_b.reshape(B, S, D_B)],
                                axis=-1).astype(x.dtype)
        x = x + mixed @ w_out[l]

        x = x + 0.5 * swiglu_ffn(rmsnorm(x, ffn2_norm[l]), ffn2_w_in[l], ffn2_w_out[l])
    return x


_drawn_inputs = setup_inputs


def setup_inputs(seed=0):
    import zlib

    import numpy as np

    out = dict(_drawn_inputs(seed))
    spreads = {}
    factors = {'ffn1_norm': 6.069,
     'mix_norm': 6.224,
     'q_norm_a': 8.0,
     'k_norm_a': 8.0,
     'q_norm_b': 8.0,
     'k_norm_b': 8.0,
     'ffn2_norm': 7.337}
    for name, (base, spread) in spreads.items():
        noise = np.random.default_rng([zlib.crc32(name.encode()), seed]).standard_normal(out[name].shape)
        drawn = base * np.exp(spread * noise) if base else spread * noise
        out[name] = __import__('jax').numpy.asarray(drawn.astype(out[name].dtype))
    for name, factor in factors.items():
        out[name] = (out[name] * factor).astype(out[name].dtype)
    return out
```

```python
import math
from contextlib import ExitStack

import numpy as np
import concourse.bass as bass
from concourse import mybir

P = 128
D_MODEL, SEQ, HEAD_DIM = 2048, 256, 128
D_FF = ((8 * D_MODEL // 3 + 127) // 128) * 128
KT = D_MODEL // P
FT = D_FF // P
TB = SEQ // P
H_A = H_B = 8
N_HEADS = H_A + H_B
D_A = H_A * HEAD_DIM
EPS = 1e-6
SCALE = HEAD_DIM ** -0.5
MASKED = -1e30
NUM_BUCKETS, MAX_DISTANCE = 32, 2048
PATTERNS = ((128, 1), (512, 4), (2048, 16))
VEC = 384

HALF = KT // 2
OUT_TILES = [min(KT, FT - KT * t) for t in range(3)]
RAW_SLOTS, HALF_SLOTS = 3, 4
UNROLL = 6

FFN_IN = [0, 0]
FFN_OUT = [0, 0]
FFN_OUT[0] = 2 * FT
HEADS = FFN_OUT[0] + 3 * KT
W_OUT = HEADS + 3 * N_HEADS
FFN_IN[1] = W_OUT + KT
FFN_OUT[1] = FFN_IN[1] + 2 * FT
END = FFN_OUT[1] + 3 * KT
B_FFN_IN, B_FFN_OUT = [0, 0], [0, 0]
B_FFN_OUT[0] = 2 * FT
B_HEADS = B_FFN_OUT[0] + KT
B_W_OUT = B_HEADS + 3 * N_HEADS
B_FFN_IN[1] = B_W_OUT + KT
B_FFN_OUT[1] = B_FFN_IN[1] + 2 * FT


class Count:

    def __init__(self, off, reg=None, step=0):
        self.off, self.reg, self.step = off, reg, step

    def __add__(self, k):
        return Count(self.off + k, self.reg, self.step)

    def __sub__(self, k):
        return self + (-k)

    def __mul__(self, k):
        return Count(self.off * k, self.reg, self.step * k)

    def __floordiv__(self, k):
        assert self.step % k == 0
        return Count(self.off // k, self.reg, self.step // k)

    def __mod__(self, k):
        assert self.step % k == 0
        return self.off % k

    def exists(self):
        return self.off >= 0

    def value(self):
        return self.off if self.reg is None or not self.step else self.reg * self.step + self.off


def wait(eng, sem, count):
    if isinstance(count, int):
        count = Count(count)
    assert count.reg is None or count.off >= 0
    if count.reg is None and count.off <= 0:
        return
    eng.wait_ge(sem, count.value())


def cols(index, size):
    return bass.ds((index * size).value(), size)


def layer(nc, io, out):
    f32, f32r = mybir.dt.float32, mybir.dt.float32r
    ALU, ACT, AX = mybir.AluOpType, mybir.ActivationFunctionType, mybir.AxisListType
    ctx = ExitStack()
    with ctx:
        base = -(-nc.sbuf_base // 64) * 64
        place = [base]

        def sb(name, shape, dtype=f32):
            size = -(-int(np.prod(shape[1:])) * 4 // 32) * 32
            t = nc.alloc_sbuf_tensor_at(name, shape, dtype, offset=place[0])
            place[0] += size
            return t

        xT = sb("xT", [P, KT * SEQ])
        xs_at = place[0]
        xs = sb("xs", [P, KT, 2, SEQ], f32r)
        raw = sb("raw", [P, RAW_SLOTS, KT, P])
        whi = sb("whi", [P, HALF_SLOTS, HALF, P], f32r)
        wlo = sb("wlo", [P, HALF_SLOTS, HALF, P], f32r)
        main = sb("main", [P, 2, SEQ])
        total = sb("total", [P, 2, SEQ])
        xsq = sb("xsq", [P, 2, SEQ])
        ssq = sb("ssq", [P, SEQ])
        rstd = sb("rstd", [P, SEQ])
        gate, silu, up, act_f = (sb(n, [P, SEQ]) for n in ("gate", "silu", "up", "act_f"))
        ident = sb("ident", [P, P])
        gain_rows = sb("gain_rows", [KT, P])
        gain_rows2 = sb("gain_rows2", [2 * KT + 4, P])
        gains = sb("gains", [P, 64])
        gqk = sb("gqk", [P, 2])
        inv_d = sb("inv_d", [P, 1])
        inv_h = sb("inv_h", [P, 1])
        neg_half = sb("neg_half", [P, 4])
        xss4 = sb("xss4", [P, TB, 4])
        xss = sb("xss", [P, TB])
        xms = sb("xms", [P, TB])
        xrs = sb("xrs", [P, TB])
        f_bias = sb("f_bias", [H_B, 1])
        wf = sb("wf", [P, KT, H_B])
        wf_hi = sb("wf_hi", [P, KT, H_B], f32r)
        wf_lo = sb("wf_lo", [P, KT, H_B], f32r)
        vec = sb("vec", [H_A, VEC])
        arena = place[0]
        act = sb("act", [P, FT, 2, SEQ], f32r)
        ends = [place[0]]
        place[0] = arena
        x_in = sb("x_in", [P, TB, D_MODEL])
        x_in_sq = sb("x_in_sq", [P, 4, TB, D_MODEL // 4])
        table = sb("table", [NUM_BUCKETS, H_A])
        one_hot = sb("one_hot", [NUM_BUCKETS, VEC])
        vec_mask = sb("vec_mask", [H_A, VEC])
        ends.append(place[0])
        place[0] = arena
        mix = sb("mix", [P, N_HEADS, 2, SEQ], f32r)
        dmat = sb("dmat", [P, N_HEADS * 3 * P])
        mult = sb("mult", [P, 3 * P])
        causal = sb("causal", [P, 3 * P])
        upper = sb("upper", [P, TB, SEQ])
        qT, kT, vT, kn = (sb(n, [P, 2, SEQ]) for n in ("qT", "kT", "vT", "kn"))
        vN = sb("vN", [P, 2, TB, P])
        hsq = sb("hsq", [P, 2, 2, SEQ])
        logit, expd, prob, pnorm, probT = (sb(n, [P, 3 * P]) for n in ("logit", "expd", "prob", "pnorm", "probT"))
        f_main, f_tot, f_exp = (sb(n, [H_B, SEQ]) for n in ("f_main", "f_tot", "f_exp"))
        nlfT = sb("nlfT", [P, TB, H_B])
        ncum = sb("ncum", [P, TB, H_B])
        hms = sb("hms", [P, 4])
        hrs = sb("hrs", [P, 2, 4])
        mx, nmx, den, rden = (sb(n, [P, TB]) for n in ("mx", "nmx", "den", "rden"))
        ends.append(place[0])
        assert max(ends) <= nc.sbuf_usable_end, (ends, nc.sbuf_usable_end)
        place[0] = xs_at
        x_final = sb("x_final", [P, 2, SEQ])
        ost = sb("ost", [P, 2, TB, P])

        def ps(name):
            return ctx.enter_context(nc.psum_tensor(name, [P, 512], f32))

        acc = [ps("acc0"), ps("acc1")]
        ps_st, ps_bc, ps_v, ps_l, ps_pt, ps_o = (ps(n) for n in ("ps_st", "ps_bc", "ps_v", "ps_l", "ps_pt", "ps_o"))
        x_banks = [ps_bc, ps_v, ps_l, ps_pt]
        row_banks = [ps_pt, ps_o]
        o_banks = [ps_v, ps_l]
        scratch = nc.dram_tensor("bias_vectors", (H_A, P, VEC), f32).ap()

        def sem(name):
            return ctx.enter_context(nc.semaphore(name))

        raw_full = [sem(f"raw_full{s}") for s in range(RAW_SLOTS)]
        weights_hi, weights_lo, weights_used = sem("weights_hi"), sem("weights_lo"), sem("weights_used")
        main_copied, block_summed = sem("main_copied"), sem("block_summed")
        gate_scaled, silu_done, up_scaled, act_done, act_hi, act_ready = (
            sem(n) for n in ("gate_scaled", "silu_done", "up_scaled", "act_done", "act_hi", "act_ready"))
        x_updated, x_hi, x_ready, x_squared, ssq_added = (
            sem(n) for n in ("x_updated", "x_hi", "x_ready", "x_squared", "ssq_added"))
        xms_psum, xms_ready, xrs_ready, rstd_psum, rstd_ready = (
            sem(n) for n in ("xms_psum", "xms_ready", "xrs_ready", "rstd_psum", "rstd_ready"))
        x_loaded = [sem(f"x_loaded{c}") for c in range(4)]
        ident_zero, ident_ready, small_set, gains_loaded, gains2_loaded, gains_psum, gains_ready, gqk_ready, xss_ready = (
            sem(n) for n in ("ident_zero", "ident_ready", "small_set", "gains_loaded", "gains2_loaded", "gains_psum",
                             "gains_ready", "gqk_ready", "xss_ready"))
        xss4_ready, table_warm = sem("xss4_ready"), sem("table_warm")
        f_loaded, wf_hi_ready, wf_ready = sem("f_loaded"), sem("wf_hi_ready"), sem("wf_ready")
        x_psum = sem("x_psum")
        vec_loaded, vec_psum, vec_ready, vec_stored = (
            sem(n) for n in ("vec_loaded", "vec_psum", "vec_ready", "vec_stored"))
        mixer_loaded = sem("mixer_loaded")
        f_psum, f_copied, f_step, f_exped, nlf_ready, nlfT_psum, nlfT_ready, ncum_psum, ncum_ready, row_psum, d_built = (
            sem(n) for n in ("f_psum", "f_copied", "f_step", "f_exped", "nlf_ready", "nlfT_psum", "nlfT_ready",
                             "ncum_psum", "ncum_ready", "row_psum", "d_built"))
        q_ready, q_squared, k_ready, k_squared, v_ready = (
            sem(n) for n in ("q_ready", "q_squared", "k_ready", "k_squared", "v_ready"))
        hms_psum, hms_ready, hrs_ready, hrs_psum, kn_ready = (
            sem(n) for n in ("hms_psum", "hms_ready", "hrs_ready", "hrs_psum", "kn_ready"))
        vN_psum, vN_ready, logit_psum, logit_ready, max_ready, nmax_ready, exp_ready = (
            sem(n) for n in ("vN_psum", "vN_ready", "logit_psum", "logit_ready", "max_ready", "nmax_ready", "exp_ready"))
        den_ready, rden_ready, prob_ready, probT_psum, probT_ready, o_psum, mix_hi, mix_ready = (
            sem(n) for n in ("den_ready", "rden_ready", "prob_ready", "probT_psum", "probT_ready", "o_psum", "mix_hi", "mix_ready"))
        ost_psum, ost_ready = sem("ost_psum"), sem("ost_ready")
        stored = [sem("stored0"), sem("stored1")]

        def x_tile(j):
            return xT[:, cols(j, SEQ)]

        def x_split(j, part):
            return xs[:, bass.ds(j.value(), 1), part, :].rearrange("p a s -> p (a s)")

        def d_tile(head, lo, hi):
            at = (head // 2 + (H_A if head % 2 else 0)) * (3 * P)
            return dmat[:, bass.ds((at + lo).value(), hi - lo)]

        def mix_tile(head, part):
            at = head // 2 + (H_A if head % 2 else 0)
            return mix[:, bass.ds(at.value(), 1), part, :].rearrange("p a s -> p (a s)")

        def half_tiles(h_in_block):
            t, half = h_in_block // 2, h_in_block % 2
            return min(HALF, OUT_TILES[t] - HALF * half)

        block = ctx.enter_context(nc.Block())

        @block.sync
        def _(sp):
            def piece(n, src, tiles=KT):
                wait(sp, weights_lo, (n - RAW_SLOTS + 1) * 2)
                sp.dma_start(raw[:, n % RAW_SLOTS, 0:tiles, :], src).then_inc(raw_full[n % RAW_SLOTS], 16)

            sp.dma_start(gain_rows[:], io["ffn1_norm"][0].rearrange("(k p) -> k p", p=P)).then_inc(gains_loaded, 16)
            x_rows = io["x"][0].rearrange("(b p) d -> p b d", p=P)
            for c in range(4):
                w = D_MODEL // 4
                sp.dma_start(x_in[:, :, c * w:(c + 1) * w], x_rows[:, :, c * w:(c + 1) * w]).then_inc(x_loaded[c], 16)
            for u in range(2):
                w_in = io[f"ffn{u + 1}_w_in"][0].rearrange("(k p) f -> p k f", p=P)
                w_out = io[f"ffn{u + 1}_w_out"][0].rearrange("(t p) d -> p t d", p=P)

                def in_piece(q, n):
                    c = (q // 2) * P + (D_FF if q % 2 else 0)
                    piece(n, w_in[:, :, bass.ds(c.value(), P)])

                for q in range(2):
                    in_piece(Count(q), Count(FFN_IN[u] + q))
                with sp.Fori(0, (2 * FT - 2) // UNROLL) as i:
                    for q in range(2, 2 + UNROLL):
                        in_piece(Count(q, i, UNROLL), Count(FFN_IN[u] + q, i, UNROLL))
                with sp.Fori(0, KT // 2) as i:
                    for q in range(UNROLL):
                        j, t = Count(q // 3, i, 2), q % 3
                        piece(Count(FFN_OUT[u] + q, i, UNROLL),
                              w_out[:, KT * t:KT * t + OUT_TILES[t], cols(j, P)], OUT_TILES[t])
                if u == 0:
                    w_mix = io["w_in"][0].rearrange("(k p) f -> p k f", p=P)
                    with sp.Fori(0, N_HEADS // 2) as i:
                        for q in range(UNROLL):
                            c = Count((q // 3) * 3 * D_A + (q % 3) * D_A, i, HEAD_DIM)
                            piece(Count(HEADS + q, i, UNROLL), w_mix[:, :, bass.ds(c.value(), P)])
                    w_o = io["w_out"][0].rearrange("(k p) d -> p k d", p=P)
                    for j in range(4):
                        piece(Count(W_OUT + j), w_o[:, :, j * P:(j + 1) * P])
                    with sp.Fori(0, (KT - 4) // UNROLL) as i:
                        for q in range(UNROLL):
                            piece(Count(W_OUT + 4 + q, i, UNROLL), w_o[:, :, cols(Count(4 + q, i, UNROLL), P)])

        @block.gpsimd
        def _(pool):
            pool.memset(inv_d[:], 1.0 / D_MODEL).then_inc(small_set, 1)
            pool.memset(inv_h[:], 1.0 / HEAD_DIM).then_inc(small_set, 1)
            pool.memset(neg_half[:], -0.5).then_inc(small_set, 1)
            pool.memset(ident[:], 0.0).then_inc(ident_zero, 1)
            pool.wait_ge(ident_zero, 1)
            pool.affine_select(out=ident[:], in_=ident[:], compare_op=ALU.not_equal, fill=1.0, base=0,
                               pattern=[[-1, P]], channel_multiplier=1).then_inc(ident_ready, 1)
            pool.dma_start(table[:], io["rel_bias_table"]).then_inc(vec_loaded, 16)
            pool.dma_start(one_hot[:], io["c_one_hot"]).then_inc(vec_loaded, 16)
            pool.dma_start(vec_mask[:], io["c_vec_mask"]).then_inc(vec_loaded, 16)
            for s, name in enumerate(("mix_norm", "ffn2_norm")):
                pool.dma_start(gain_rows2[s * KT:(s + 1) * KT, :], io[name][0].rearrange("(k p) -> k p", p=P)).then_inc(gains2_loaded, 16)
            for s, name in enumerate(("q_norm_a", "k_norm_a", "q_norm_b", "k_norm_b")):
                pool.dma_start(gain_rows2[2 * KT + s:2 * KT + s + 1, :], io[name]).then_inc(gains2_loaded, 16)
            pool.dma_start(wf[:], io["w_in"][0].rearrange("(k p) f -> p k f", p=P)[:, :, 6 * D_A:6 * D_A + H_B]).then_inc(f_loaded, 16)
            pool.dma_start(f_bias[:], io["forget_bias"].rearrange("a h -> h a")).then_inc(f_loaded, 16)

            def add_square(X, j0):
                wait(pool, x_squared, X + 1)
                if j0:
                    wait(pool, xms_psum, X.off // KT)
                    pool.tensor_copy(ssq[:], xsq[:, X % 2, :]).then_inc(ssq_added, 1)
                else:
                    wait(pool, ssq_added, X)
                    pool.tensor_tensor(ssq[:], ssq[:], xsq[:, X % 2, :], ALU.add).then_inc(ssq_added, 1)

            def x_power(s):
                wait(pool, xms_ready, s + 1)
                pool.tensor_tensor(xrs[:], xms[:], neg_half[:, 0:TB], ALU.pow).then_inc(xrs_ready, 1)

            def head_power(H):
                wait(pool, hms_ready, H + 1)
                pool.tensor_tensor(hrs[:, H % 2, :], hms[:], neg_half[:], ALU.pow).then_inc(hrs_ready, 1)

            pool.wait_ge(small_set, 3)
            x_power(0)
            pool.wait_ge(vec_ready, 1)
            pool.dma_start(scratch, vec[:].rearrange("h (a v) -> h a v", a=1).to_broadcast([H_A, P, VEC])).then_inc(vec_stored, 16)
            for s in (1, 2):
                first = KT * (s - 1)
                add_square(Count(first), True)
                add_square(Count(first + 1), False)
                with pool.Fori(0, KT // 2 - 1) as i:
                    for j in range(2):
                        add_square(Count(first + 2 + j, i, 2), False)
                if s == 1:
                    pool.wait_ge(weights_used, 2 * HEADS)
                    pool.wait_ge(vec_stored, 16)
                    pool.dma_start(mult[:], io["c_mult"]).then_inc(mixer_loaded, 16)
                    pool.dma_start(causal[:], io["c_causal"]).then_inc(mixer_loaded, 16)
                    pool.dma_start(upper[:], io["c_upper"]).then_inc(mixer_loaded, 16)
                    d_a = dmat[:, 0:H_A * 3 * P].rearrange("p (h c) -> p h c", h=H_A)
                    for b in range(TB):
                        src = bass.AP(tensor=scratch.tensor, offset=SEQ - 1 - b * P,
                                      ap=[[VEC - 1, P], [P * VEC, H_A], [1, (b + 1) * P]])
                        pool.dma_start(d_a[:, :, b * P:b * P + (b + 1) * P], src).then_inc(mixer_loaded, 16)
                x_power(s)
                if s == 1:
                    with pool.Fori(0, N_HEADS // 2) as i:
                        for g in range(2):
                            head_power(Count(g, i, 2))

        @block.tensor
        def _(pe):
            mm = nc.tensor.matmul

            def pair(bank, slot, kk, moving, first, last, m=P):
                mm(bank[:, 0:2 * SEQ], whi[:, slot, kk, :], moving.rearrange("p a s -> p (a s)"), start=first, stop=False,
                   skip_group_check=True)
                return mm(bank[:, SEQ:2 * SEQ], wlo[:, slot, kk, :], moving[:, 0, :], start=False, stop=last,
                          skip_group_check=True)

            def half(h, bank, tiles, k0, k_total, moving, before=None):
                wait(pe, weights_lo, h + 1)
                for kk in range(tiles):
                    k = k0 + kk
                    if before:
                        before(k)
                    last = pair(bank, h % HALF_SLOTS, kk, moving[:, k, :, :], k == 0, k == k_total - 1)
                last.then_inc(weights_used, 1)

            def in_block(n, b, moving, before=None, between=None):
                wait(pe, block_summed, b - 1)
                half(n * 2, acc[b % 2], HALF, 0, KT, moving, before)
                if between:
                    between()
                half(n * 2 + 1, acc[b % 2], HALF, HALF, KT, moving, before)

            def out_block(n, b, before=None):
                wait(pe, block_summed, b - 1)
                for h in range(6):
                    half(n * 2 + h, acc[b % 2], half_tiles(h), HALF * h, FT, act, before)

            def x_stats(s):
                wait(pe, ssq_added, KT * s)
                for b in range(TB):
                    last = mm(ps_st[:, b:b + 1], ssq[:, b * P:(b + 1) * P], inv_d[:], start=True, stop=True)
                last.then_inc(xms_psum, 1)

            def x_spread(s):
                wait(pe, xrs_ready, s + 1)
                for b in range(TB):
                    last = mm(ps_bc[:, b * P:(b + 1) * P], xrs[:, b:b + 1].to_broadcast([P, P]), ident[:],
                              start=True, stop=True, skip_group_check=True)
                last.then_inc(rstd_psum, 1)

            pe.wait_ge(gains_loaded, 16)
            pe.wait_ge(ident_ready, 1)
            nc.tensor.transpose(ps_st[:, 0:KT], gain_rows[:], ident[0:KT, 0:KT]).then_inc(gains_psum, 1)
            for j in range(KT):
                if j % 4 == 0:
                    pe.wait_ge(x_loaded[j // 4], 16)
                wait(pe, x_updated, j - 3)
                for b in range(TB):
                    last = nc.tensor.transpose(x_banks[j % 4][:, b * P:(b + 1) * P], x_in[:, b, j * P:(j + 1) * P], ident[:])
                last.then_inc(x_psum, 1)

            def small_products():
                pe.wait_ge(gains2_loaded, 6 * 16)
                pe.wait_ge(gains_ready, 1)
                rows = 2 * KT + 4
                nc.tensor.transpose(ps_st[:, 0:rows], gain_rows2[:], ident[0:rows, 0:rows]).then_inc(gains_psum, 1)
                pe.wait_ge(vec_loaded, 48)
                mm(ps_o[0:H_A, 0:VEC], table[:], one_hot[:], start=True, stop=True).then_inc(vec_psum, 1)

            def ffn_in(u, before, s):
                n, b = FFN_IN[u], B_FFN_IN[u]
                in_block(Count(n), Count(b), xs, before)
                if u:
                    x_stats(s)
                in_block(Count(n + 1), Count(b + 1), xs, between=lambda: x_spread(s))
                with pe.Fori(0, (2 * FT - 2) // UNROLL) as i:
                    for q in range(2, 2 + UNROLL):
                        in_block(Count(n + q, i, UNROLL), Count(b + q, i, UNROLL), xs)

            def tile_ready(first):
                return lambda k: wait(pe, x_ready, first + k + 1)

            small_products()

            ffn_in(0, tile_ready(0), 0)
            out_block(Count(FFN_OUT[0]), Count(B_FFN_OUT[0]), lambda k: wait(pe, act_ready, k + 1))
            out_block(Count(FFN_OUT[0] + 3), Count(B_FFN_OUT[0] + 1))
            with pe.Fori(0, KT // 2 - 1) as i:
                for j in range(2):
                    out_block(Count(FFN_OUT[0] + 6 + 3 * j, i, 6), Count(B_FFN_OUT[0] + 2 + j, i, 2))

            def head_stats(H):
                if not H.exists():
                    return
                wait(pe, q_squared, H + 1)
                wait(pe, k_squared, H + 1)
                for c in range(4):
                    last = mm(ps_st[:, c:c + 1], hsq[:, H % 2, c // 2, (c % 2) * P:(c % 2 + 1) * P], inv_h[:],
                              start=True, stop=True)
                last.then_inc(hms_psum, 1)

            def k_spread_v_turn(H):
                if not H.exists():
                    return
                wait(pe, hrs_ready, H + 1)
                for b in range(TB):
                    last = mm(ps_bc[:, b * P:(b + 1) * P], hrs[:, H % 2, 2 + b:3 + b].to_broadcast([P, P]), ident[:],
                              start=True, stop=True, skip_group_check=True)
                last.then_inc(hrs_psum, 1)
                wait(pe, v_ready, H + 1)
                wait(pe, vN_ready, H)
                for b in range(TB):
                    last = nc.tensor.transpose(ps_v[:, b * P:(b + 1) * P], vT[:, H % 2, b * P:(b + 1) * P], ident[:])
                last.then_inc(vN_psum, 1)

            def logits(H):
                if not H.exists():
                    return
                wait(pe, kn_ready, H + 1)
                mm(ps_l[:, 0:P], qT[:, H % 2, 0:P], kn[:, H % 2, 0:P], start=True, stop=True, skip_group_check=True)
                mm(ps_l[:, P:3 * P], qT[:, H % 2, P:2 * P], kn[:, H % 2, :], start=True, stop=True,
                   skip_group_check=True).then_inc(logit_psum, 1)

            def prob_turn(H):
                if not H.exists():
                    return
                wait(pe, prob_ready, H + 1)
                for c in range(3):
                    last = nc.tensor.transpose(ps_pt[:, c * P:(c + 1) * P], pnorm[:, c * P:(c + 1) * P], ident[:])
                last.then_inc(probT_psum, 1)

            def weighted(H):
                if not H.exists():
                    return
                wait(pe, probT_ready, H + 1)
                wait(pe, vN_ready, H + 1)
                wait(pe, mix_ready, H)
                mm(ps_o[:, 0:SEQ], vN[:, H % 2, 0, :], probT[:, 0:SEQ], start=True, stop=False, skip_group_check=True)
                mm(ps_o[:, P:SEQ], vN[:, H % 2, 1, :], probT[:, SEQ:3 * P], start=False, stop=True,
                   skip_group_check=True).then_inc(o_psum, 1)

            def forget_product():
                pe.wait_ge(wf_ready, 1)
                for k in range(KT):
                    mm(ps_l[0:H_B, 0:2 * SEQ], wf_hi[:, k, :], xs[:, k, :, :].rearrange("p a s -> p (a s)"),
                       start=k == 0, stop=False, skip_group_check=True)
                    last = mm(ps_l[0:H_B, SEQ:2 * SEQ], wf_lo[:, k, :], xs[:, k, 0, :], start=False, stop=k == KT - 1,
                              skip_group_check=True)
                last.then_inc(f_psum, 1)

            def forget_turn():
                pe.wait_ge(nlf_ready, 1)
                for b in range(TB):
                    last = nc.tensor.transpose(ps_v[:, b * H_B:(b + 1) * H_B], f_tot[:, b * P:(b + 1) * P], ident[0:H_B, 0:H_B])
                last.then_inc(nlfT_psum, 1)

            def forget_sums():
                pe.wait_ge(nlfT_ready, 1)
                pe.wait_ge(mixer_loaded, 5 * 16)
                mm(ps_st[:, 0:H_B], upper[:, 0, 0:P], nlfT[:, 0, :], start=True, stop=True, skip_group_check=True)
                mm(ps_st[:, H_B:2 * H_B], upper[:, 0, P:SEQ], nlfT[:, 0, :], start=True, stop=False, skip_group_check=True)
                mm(ps_st[:, H_B:2 * H_B], upper[:, 1, P:SEQ], nlfT[:, 1, :], start=False, stop=True,
                   skip_group_check=True).then_inc(ncum_psum, 1)
                for h in range(H_B):
                    bank = row_banks[h % 2]
                    wait(pe, d_built, h - 1)
                    mm(bank[:, 0:SEQ], nlfT[:, 0, h:h + 1].to_broadcast([P, P]), upper[:, 0, :], start=True, stop=False,
                       skip_group_check=True)
                    mm(bank[:, P:SEQ], nlfT[:, 1, h:h + 1].to_broadcast([P, P]), upper[:, 1, P:SEQ], start=False, stop=True,
                       skip_group_check=True).then_inc(row_psum, 1)

            def head(n, b, H, before=None, forget=False):
                in_block(n, b, xs, before)
                if forget:
                    x_stats(1)
                    forget_product()
                    x_spread(1)
                head_stats(H - 1)
                in_block(n + 1, b + 1, xs)
                if forget:
                    forget_turn()
                k_spread_v_turn(H - 1)
                prob_turn(H - 2)
                in_block(n + 2, b + 2, xs)
                if forget:
                    forget_sums()
                logits(H - 1)
                weighted(H - 2)

            for H in range(4):
                head(Count(HEADS + 3 * H), Count(B_HEADS + 3 * H), Count(H), tile_ready(KT) if H == 0 else None, H == 0)
            with pe.Fori(0, N_HEADS // 2 - 2) as i:
                for g in range(2):
                    head(Count(HEADS + 12 + 3 * g, i, 6), Count(B_HEADS + 12 + 3 * g, i, 6), Count(4 + g, i, 2))

            last_head = N_HEADS - 1

            def part(j, tiles, first=False):
                h0 = 2 * (W_OUT + j)
                for k in tiles:
                    if first and k == tiles[0]:
                        wait(pe, block_summed, B_W_OUT + j - 1)
                        wait(pe, weights_lo, h0 + 2)
                    done = pair(acc[(B_W_OUT + j) % 2], (h0 + k // HALF) % HALF_SLOTS, k % HALF, mix[:, k, :, :],
                                first and k == tiles[0], k == KT - 1)
                    if k in (HALF - 1, KT - 1):
                        done.then_inc(weights_used, 1)

            head_stats(Count(last_head))
            pe.wait_ge(mix_ready, last_head - 3)
            part(0, [0, 1, 2, 3, 4, 5, 8, 9, 10, 11, 12, 13], True)
            pe.wait_ge(mix_ready, last_head - 1)
            part(0, [6, 14])
            k_spread_v_turn(Count(last_head))
            prob_turn(Count(last_head - 1))
            part(1, [0, 1, 2, 3, 4, 5, 6], True)
            logits(Count(last_head))
            weighted(Count(last_head - 1))
            part(1, [8, 9, 10, 11, 12, 13, 14])
            prob_turn(Count(last_head))
            weighted(Count(last_head))
            pe.wait_ge(mix_ready, last_head + 1)
            part(0, [7, 15])
            part(1, [7, 15])
            for j in range(2, 4):
                in_block(Count(W_OUT + j), Count(B_W_OUT + j), mix)
            with pe.Fori(0, (KT - 4) // UNROLL) as i:
                for q in range(4, 4 + UNROLL):
                    in_block(Count(W_OUT + q, i, UNROLL), Count(B_W_OUT + q, i, UNROLL), mix)

            def out_turn(j):
                wait(pe, x_updated, j + 3 * KT + 1)
                wait(pe, ost_ready, j - 1)
                for b in range(TB):
                    last = nc.tensor.transpose(o_banks[j % 2][:, b * P:(b + 1) * P],
                                               x_final[:, j % 2, b * P:(b + 1) * P], ident[:])
                last.then_inc(ost_psum, 1)

            ffn_in(1, tile_ready(2 * KT), 2)
            out_block(Count(FFN_OUT[1]), Count(B_FFN_OUT[1]), lambda k: wait(pe, act_ready, FT + k + 1))
            out_block(Count(FFN_OUT[1] + 3), Count(B_FFN_OUT[1] + 1))
            out_turn(Count(0))
            with pe.Fori(0, KT // 2 - 1) as i:
                for j in range(2):
                    out_block(Count(FFN_OUT[1] + 6 + 3 * j, i, 6), Count(B_FFN_OUT[1] + 2 + j, i, 2))
                    out_turn(Count(1 + j, i, 2))
            out_turn(Count(KT - 1))

        @block.scalar
        def _(act_e):
            A = nc.scalar.activation

            def split(h, tiles=HALF):
                n = h // 2
                slot, first = n % RAW_SLOTS, HALF * (h % 2)
                wait(act_e, raw_full[slot], (n // RAW_SLOTS + 1) * 16)
                wait(act_e, weights_used, h - HALF_SLOTS + 1)
                A(whi[:, h % HALF_SLOTS, 0:tiles, :], raw[:, slot, first:first + tiles, :], ACT.Copy).then_inc(weights_hi, 1)

            def copy_main(b, used):
                wait(act_e, weights_used, used)
                A(main[:, b % 2, :], acc[b % 2][:, 0:SEQ], ACT.Copy).then_inc(main_copied, 1)

            def x_split_hi(X, j):
                wait(act_e, x_updated, X + 1)
                A(x_split(j, 0), x_tile(j), ACT.Copy, scale=gains[:, bass.ds(X.value(), 1)]).then_inc(x_hi, 1)

            def x_square_free(X):
                wait(act_e, ssq_added, X - (KT + 1))

            def x_square(X, j):
                A(xsq[:, X % 2, :], x_tile(j), ACT.Square).then_inc(x_squared, 1)

            def copy_rstd(s):
                wait(act_e, rstd_psum, s + 1)
                A(rstd[:], ps_bc[:, 0:SEQ], ACT.Copy).then_inc(rstd_ready, 1)

            act_e.wait_ge(small_set, 2)
            A(xss4[:, 0, 0:1], inv_h[:], ACT.Square).then_inc(table_warm, 1)
            act_e.wait_ge(table_warm, 1)
            act_e.wait_ge(gains_ready, 1)
            for j in range(KT):
                x_split_hi(Count(j), Count(j))
                if j in (6, 11):
                    split(Count(j // 7))
                if j >= KT // 2:
                    c, b = (j - KT // 2) // TB, j % TB
                    w = D_MODEL // 4
                    act_e.wait_ge(x_loaded[c], 16)
                    A(x_in_sq[:, c, b, :], x_in[:, b, c * w:(c + 1) * w], ACT.Square, accum_out=xss4[:, b, c:c + 1]).then_inc(xss4_ready, 1)
            split(Count(2))
            split(Count(3))
            act_e.wait_ge(f_loaded, 32)
            A(wf_hi[:], wf[:], ACT.Copy).then_inc(wf_hi_ready, 1)

            def hidden_early(u, p):
                copy_main(p + B_FFN_IN[u], (p + FFN_IN[u] + 1) * 2)

            def hidden_late(u, p, is_up):
                F = p // 2 + u * FT
                if is_up:
                    wait(act_e, act_done, F + 1)
                    A(act[:, bass.ds((p // 2).value(), 1), 0, :].rearrange("p a s -> p (a s)"), act_f[:], ACT.Copy).then_inc(act_hi, 1)
                else:
                    wait(act_e, gate_scaled, F + 1)
                    A(silu[:], gate[:], ACT.Silu).then_inc(silu_done, 1)

            def out_late(u, j):
                if u == 0:
                    x_square_free(j + KT)
                    x_split_hi(j + KT, j)
                    x_square(j + KT, j)
                else:
                    store(j - 1)

            def store(j):
                if not j.exists():
                    return
                wait(act_e, ost_psum, j + 1)
                wait(act_e, stored[j % 2], (j // 2) * 16)
                A(ost[:, j % 2, :, :], o_banks[j % 2][:, 0:SEQ].rearrange("p (b d) -> p b d", b=TB), ACT.Copy).then_inc(ost_ready, 1)
                wait(act_e, ost_ready, j + 1)
                act_e.dma_start(out[0].rearrange("(b p) d -> p b d", p=P)[:, :, cols(j, P)], ost[:, j % 2, :, :]).then_inc(stored[j % 2], 16)

            def swiglu(u):
                copy_rstd(2 * u)
                with act_e.Fori(0, (2 * FT - 2) // UNROLL) as i:
                    for q in range(2, 2 + UNROLL):
                        n, p = Count(FFN_IN[u] + q, i, UNROLL), Count(q - 2, i, UNROLL)
                        split(n * 2)
                        hidden_early(u, p)
                        split(n * 2 + 1)
                        hidden_late(u, p, q % 2)
                for q in range(UNROLL):
                    n = Count(FFN_OUT[u] + q)
                    split(n * 2, half_tiles(q % 3 * 2))
                    if q < 2:
                        hidden_early(u, Count(2 * FT - 2 + q))
                    if q == 4:
                        copy_main(Count(B_FFN_OUT[u]), Count(FFN_OUT[u] + 3) * 2)
                    split(n * 2 + 1, half_tiles(q % 3 * 2 + 1))
                    if q < 2:
                        hidden_late(u, Count(2 * FT - 2 + q), q)
                    if q == 4:
                        out_late(u, Count(0))
                with act_e.Fori(0, KT // 2 - 1) as i:
                    for q in range(UNROLL, 2 * UNROLL):
                        n = Count(FFN_OUT[u] + q, i, UNROLL)
                        j = Count((q - 4) // 3, i, 2)
                        split(n * 2, half_tiles(q % 3 * 2))
                        if q % 3 == 1:
                            copy_main(j + B_FFN_OUT[u], (j * 3 + (FFN_OUT[u] + 3)) * 2)
                        split(n * 2 + 1, half_tiles(q % 3 * 2 + 1))
                        if q % 3 == 1:
                            out_late(u, j)

            def last_out(u):
                copy_main(Count(B_FFN_OUT[u] + KT - 1), Count(FFN_OUT[u] + 3 * KT) * 2)

            swiglu(0)

            def exps(H):
                if not H.exists():
                    return
                wait(act_e, nmax_ready, H + 1)
                for b in range(TB):
                    c = slice(b * P, b * P + (b + 1) * P)
                    last = A(expd[:, c], logit[:, c], ACT.Exp, bias=nmx[:, b:b + 1],
                             **({"accum_out": den[:, b:b + 1]} if H % 2 else {}))
                last.then_inc(exp_ready, 1)

            def copy_vN(H):
                if H.exists():
                    wait(act_e, vN_psum, H + 1)
                    A(vN[:, H % 2, :, :], ps_v[:, 0:SEQ].rearrange("p (b d) -> p b d", b=TB), ACT.Copy).then_inc(vN_ready, 1)

            def copy_probT(H):
                if H.exists():
                    wait(act_e, probT_psum, H + 1)
                    A(probT[:], ps_pt[:, 0:3 * P], ACT.Copy).then_inc(probT_ready, 1)

            def mix_split_hi(H):
                if H.exists():
                    wait(act_e, o_psum, H + 1)
                    A(mix_tile(H, 0), ps_o[:, 0:SEQ], ACT.Copy).then_inc(mix_hi, 1)

            def head_slots(H, forget=False):
                n, b = H * 3 + (HEADS + 2), H * 3 + B_HEADS
                used = H * 6 + 2 * (HEADS + 1)
                split(n * 2)
                copy_main(b, used)
                if forget:
                    wait(act_e, f_psum, 1)
                    A(f_main[:], ps_l[0:H_B, 0:SEQ], ACT.Copy).then_inc(f_copied, 1)
                    copy_rstd(1)
                split(n * 2 + 1)
                wait(act_e, q_ready, H + 1)
                A(hsq[:, H % 2, 0, :], qT[:, H % 2, :], ACT.Square).then_inc(q_squared, 1)
                if forget:
                    wait(act_e, f_step, 4)
                    A(f_exp[:], f_main[:], ACT.Exp).then_inc(f_exped, 1)
                    wait(act_e, f_exped, 1)
                    A(f_exp[:], f_exp[:], ACT.Ln, bias=1.0).then_inc(f_exped, 1)

                split((n + 1) * 2)
                copy_main(b + 1, used + 2)
                if forget:
                    wait(act_e, nlfT_psum, 1)
                    A(nlfT[:], ps_v[:, 0:TB * H_B].rearrange("p (b h) -> p b h", b=TB), ACT.Copy).then_inc(nlfT_ready, 1)
                copy_vN(H - 1)
                copy_probT(H - 2)
                split((n + 1) * 2 + 1)
                wait(act_e, k_ready, H + 1)
                A(hsq[:, H % 2, 1, :], kT[:, H % 2, :], ACT.Square).then_inc(k_squared, 1)

                split((n + 2) * 2)
                copy_main(b + 2, used + 4)
                mix_split_hi(H - 2)
                split((n + 2) * 2 + 1)
                exps(H - 1)

            split(Count(2 * HEADS))
            split(Count(2 * HEADS + 1))
            split(Count(2 * HEADS + 2))
            last_out(0)
            split(Count(2 * HEADS + 3))
            out_late(0, Count(KT - 1))
            for H in range(4):
                head_slots(Count(H), H == 0)
            with act_e.Fori(0, N_HEADS // 2 - 2) as i:
                for g in range(2):
                    head_slots(Count(4 + g, i, 2))
            last_head = N_HEADS - 1
            copy_vN(Count(last_head))
            copy_probT(Count(last_head - 1))
            exps(Count(last_head))
            mix_split_hi(Count(last_head - 1))
            copy_probT(Count(last_head))
            mix_split_hi(Count(last_head))

            def mixed_slot(n, j):
                split(n * 2)
                copy_main(j + B_W_OUT, (j + (W_OUT + 1)) * 2)
                split(n * 2 + 1)
                x_square_free(j + 2 * KT)
                x_split_hi(j + 2 * KT, j)
                x_square(j + 2 * KT, j)

            for j in range(2):
                mixed_slot(Count(W_OUT + 2 + j), Count(j))
            with act_e.Fori(0, (KT - 4) // UNROLL) as i:
                for q in range(UNROLL):
                    mixed_slot(Count(W_OUT + 4 + q, i, UNROLL), Count(2 + q, i, UNROLL))
            for j in range(2):
                mixed_slot(Count(FFN_IN[1] + j), Count(KT - 2 + j))
            swiglu(1)
            last_out(1)
            store(Count(KT - 2))
            store(Count(KT - 1))
            for s in range(2):
                act_e.wait_ge(stored[s], 16 * KT // 2)

        @block.vector
        def _(dve):
            V = nc.vector

            def split(h, tiles=HALF):
                n = h // 2
                slot, first = n % RAW_SLOTS, HALF * (h % 2)
                wait(dve, weights_hi, h + 1)
                V.tensor_tensor(wlo[:, h % HALF_SLOTS, 0:tiles, :], raw[:, slot, first:first + tiles, :],
                                whi[:, h % HALF_SLOTS, 0:tiles, :].bitcast(f32), ALU.subtract).then_inc(weights_lo, 1)

            def add_halves(b):
                wait(dve, main_copied, b + 1)
                V.tensor_tensor(total[:, b % 2, :], main[:, b % 2, :], acc[b % 2][:, SEQ:2 * SEQ], ALU.add).then_inc(block_summed, 1)

            def scaled(b, dest, done):
                wait(dve, block_summed, b + 1)
                V.tensor_tensor(dest, total[:, b % 2, :], rstd[:], ALU.mult).then_inc(done, 1)

            def x_split_lo(X, j):
                wait(dve, x_hi, X + 1)
                wait(dve, x_updated, X + 1)
                V.scalar_tensor_tensor(x_split(j, 1), x_tile(j), gains[:, bass.ds(X.value(), 1)],
                                       x_split(j, 0).bitcast(f32), ALU.mult, ALU.subtract).then_inc(x_ready, 1)

            def x_mean_square(s):
                wait(dve, xms_psum, s)
                V.tensor_scalar(xms[:], ps_st[:, 0:TB], EPS, None, ALU.add).then_inc(xms_ready, 1)

            dve.wait_ge(gains_psum, 1)
            V.tensor_copy(gains[:, 0:KT], ps_st[:, 0:KT]).then_inc(gains_ready, 1)
            dve.wait_ge(gains_ready, 1)

            for j in range(KT + 1):
                if j < KT:
                    dve.wait_ge(x_psum, j + 1)
                    V.tensor_copy(x_tile(Count(j)), x_banks[j % 4][:, 0:SEQ]).then_inc(x_updated, 1)
                if j > 0:
                    x_split_lo(Count(j - 1), Count(j - 1))
                if j in (7, 12):
                    split(Count(j // 8))
            dve.wait_ge(xss4_ready, 8)
            V.reduce_sum(xss[:], xss4[:], AX.X).then_inc(xss_ready, 1)
            dve.wait_ge(xss_ready, 1)
            V.tensor_scalar(xms[:], xss[:], 1.0 / D_MODEL, EPS, ALU.mult, ALU.add).then_inc(xms_ready, 1)
            split(Count(2))
            split(Count(3))
            dve.wait_ge(gains_psum, 2)
            V.tensor_copy(gains[:, KT:3 * KT + 4], ps_st[:, 0:2 * KT + 4]).then_inc(gains_ready, 1)
            dve.wait_ge(gains_ready, 2)
            for g in range(2):
                q = 3 * KT + 2 * g
                V.scalar_tensor_tensor(gqk[:, g:g + 1], gains[:, q:q + 1], SCALE, gains[:, q + 1:q + 2],
                                       ALU.mult, ALU.mult).then_inc(gqk_ready, 1)
            dve.wait_ge(vec_psum, 1)
            V.tensor_tensor(vec[:], ps_o[0:H_A, 0:VEC], vec_mask[:], ALU.add).then_inc(vec_ready, 1)
            dve.wait_ge(wf_hi_ready, 1)
            V.tensor_tensor(wf_lo[:], wf[:], wf_hi[:].bitcast(f32), ALU.subtract).then_inc(wf_ready, 1)

            def hidden_early(u, p, is_up):
                b, F = p + B_FFN_IN[u], p // 2 + u * FT
                add_halves(b)
                if is_up:
                    scaled(b, up[:], up_scaled)
                    wait(dve, up_scaled, F + 1)
                    wait(dve, silu_done, F + 1)
                    V.tensor_tensor(act_f[:], silu[:], up[:], ALU.mult).then_inc(act_done, 1)
                else:
                    wait(dve, rstd_ready, 2 * u + 1)
                    scaled(b, gate[:], gate_scaled)

            def hidden_late(u, p, is_up):
                if not is_up:
                    return
                F, f = p // 2 + u * FT, p // 2
                wait(dve, act_done, F + 1)
                wait(dve, act_hi, F + 1)
                hi = act[:, bass.ds(f.value(), 1), 0, :].rearrange("p a s -> p (a s)")
                lo = act[:, bass.ds(f.value(), 1), 1, :].rearrange("p a s -> p (a s)")
                V.tensor_tensor(lo, act_f[:], hi.bitcast(f32), ALU.subtract).then_inc(act_ready, 1)

            def add_to_x(b, j, factor, dest=None):
                wait(dve, block_summed, b + 1)
                V.scalar_tensor_tensor(x_tile(j) if dest is None else dest, total[:, b % 2, :], factor, x_tile(j),
                                       ALU.mult, ALU.add).then_inc(x_updated, 1)

            def out_early(u, j):
                b = j + B_FFN_OUT[u]
                add_halves(b)
                add_to_x(b, j, 0.5, x_final[:, j % 2, :] if u else None)

            def out_late(u, j):
                if u == 0:
                    x_split_lo(j + KT, j)

            def swiglu(u):
                if u:
                    x_mean_square(2)
                with dve.Fori(0, (2 * FT - 2) // UNROLL) as i:
                    for q in range(2, 2 + UNROLL):
                        n, p = Count(FFN_IN[u] + q, i, UNROLL), Count(q - 2, i, UNROLL)
                        split(n * 2)
                        hidden_early(u, p, q % 2)
                        split(n * 2 + 1)
                        hidden_late(u, p, q % 2)
                for q in range(UNROLL):
                    n = Count(FFN_OUT[u] + q)
                    split(n * 2, half_tiles(q % 3 * 2))
                    if q < 2:
                        hidden_early(u, Count(2 * FT - 2 + q), q)
                    if q == 4:
                        out_early(u, Count(0))
                    split(n * 2 + 1, half_tiles(q % 3 * 2 + 1))
                    if q < 2:
                        hidden_late(u, Count(2 * FT - 2 + q), q)
                    if q == 4:
                        out_late(u, Count(0))
                with dve.Fori(0, KT // 2 - 1) as i:
                    for q in range(UNROLL, 2 * UNROLL):
                        n = Count(FFN_OUT[u] + q, i, UNROLL)
                        j = Count((q - 4) // 3, i, 2)
                        split(n * 2, half_tiles(q % 3 * 2))
                        if q % 3 == 1:
                            out_early(u, j)
                        split(n * 2 + 1, half_tiles(q % 3 * 2 + 1))
                        if q % 3 == 1:
                            out_late(u, j)

            swiglu(0)

            def head_mean_square(H):
                if H.exists():
                    wait(dve, hms_psum, H + 1)
                    V.tensor_scalar(hms[:], ps_st[:, 0:4], EPS, None, ALU.add).then_inc(hms_ready, 1)

            def norm_k(H):
                if H.exists():
                    wait(dve, hrs_psum, H + 1)
                    V.scalar_tensor_tensor(kn[:, H % 2, :], kT[:, H % 2, :], gqk[:, H % 2:H % 2 + 1], ps_bc[:, 0:SEQ],
                                           ALU.mult, ALU.mult).then_inc(kn_ready, 1)

            def softmax_max(H):
                if not H.exists():
                    return
                wait(dve, logit_psum, H + 1)
                for b in range(TB):
                    lo, hi = b * P, b * P + (b + 1) * P
                    last = V.scalar_tensor_tensor(logit[:, lo:hi], ps_l[:, lo:hi], hrs[:, H % 2, b:b + 1], d_tile(H, lo, hi),
                                                  ALU.mult, ALU.add)
                last.then_inc(logit_ready, 1)
                wait(dve, logit_ready, H + 1)
                for b in range(TB):
                    last = V.reduce_max(mx[:, b:b + 1], logit[:, b * P:b * P + (b + 1) * P], AX.X)
                last.then_inc(max_ready, 1)
                wait(dve, max_ready, H + 1)
                V.tensor_scalar(nmx[:], mx[:], -1.0, None, ALU.mult).then_inc(nmax_ready, 1)

            def softmax_norm(H):
                if not H.exists():
                    return
                wait(dve, exp_ready, H + 1)
                source = expd
                if H % 2 == 0:
                    source = prob
                    for b in range(TB):
                        c = slice(b * P, b * P + (b + 1) * P)
                        last = V.scalar_tensor_tensor(prob[:, c], expd[:, c], 1.0, mult[:, c], ALU.mult, ALU.mult,
                                                      accum_out=den[:, b:b + 1])
                    last.then_inc(den_ready, 1)
                    wait(dve, den_ready, H // 2 + 1)
                V.reciprocal(rden[:], den[:]).then_inc(rden_ready, 1)
                wait(dve, rden_ready, H + 1)
                for b in range(TB):
                    c = slice(b * P, b * P + (b + 1) * P)
                    last = V.tensor_scalar(pnorm[:, c], source[:, c], rden[:, b:b + 1], None, ALU.mult)
                last.then_inc(prob_ready, 1)

            def mix_split_lo(H):
                if H.exists():
                    wait(dve, mix_hi, H + 1)
                    V.tensor_tensor(mix_tile(H, 1), ps_o[:, 0:SEQ], mix_tile(H, 0).bitcast(f32), ALU.subtract).then_inc(mix_ready, 1)

            def forget_gate():
                wait(dve, f_copied, 1)
                V.tensor_tensor(f_tot[:], f_main[:], ps_l[0:H_B, SEQ:2 * SEQ], ALU.add).then_inc(f_step, 1)
                wait(dve, f_step, 1)
                V.tensor_tensor(f_tot[:], f_tot[:], rstd[0:H_B, :], ALU.mult).then_inc(f_step, 1)
                wait(dve, f_step, 2)
                V.tensor_scalar(f_tot[:], f_tot[:], f_bias[:], None, ALU.add).then_inc(f_step, 1)
                wait(dve, f_step, 3)
                V.scalar_tensor_tensor(f_main[:], f_tot[:], -1.0, f_tot[:], ALU.mult, ALU.min).then_inc(f_step, 1)
                wait(dve, f_step, 4)
                V.tensor_scalar(f_tot[:], f_tot[:], -1.0, 0.0, ALU.mult, ALU.max).then_inc(f_step, 1)

            def forget_bias_tiles():
                wait(dve, ncum_psum, 1)
                V.tensor_copy(ncum[:], ps_st[:, 0:TB * H_B].rearrange("p (b h) -> p b h", b=TB)).then_inc(ncum_ready, 1)
                wait(dve, ncum_ready, 1)
                dve.wait_ge(mixer_loaded, 5 * 16)
                for h in range(H_B):
                    wait(dve, row_psum, h + 1)
                    for b in range(TB):
                        lo, hi = b * P, b * P + (b + 1) * P
                        last = V.scalar_tensor_tensor(d_tile(Count(2 * h + 1), lo, hi), row_banks[h % 2][:, 0:(b + 1) * P],
                                                      ncum[:, b, h:h + 1], causal[:, lo:hi], ALU.subtract, ALU.add)
                    last.then_inc(d_built, 1)
                wait(dve, d_built, H_B)

            def head_slots(H, forget=False):
                n, b = H * 3 + (HEADS + 2), H * 3 + B_HEADS
                split(n * 2)
                if forget:
                    x_mean_square(1)
                head_mean_square(H - 1)
                add_halves(b)
                if forget:
                    wait(dve, rstd_ready, 2)
                scaled(b, qT[:, H % 2, :], q_ready)
                if forget:
                    forget_gate()
                split(n * 2 + 1)
                if forget:
                    wait(dve, f_step, 5)
                    wait(dve, f_exped, 2)
                    V.tensor_tensor(f_tot[:], f_tot[:], f_exp[:], ALU.add).then_inc(nlf_ready, 1)

                split((n + 1) * 2)
                norm_k(H - 1)
                add_halves(b + 1)
                scaled(b + 1, kT[:, H % 2, :], k_ready)
                split((n + 1) * 2 + 1)

                split((n + 2) * 2)
                add_halves(b + 2)
                scaled(b + 2, vT[:, H % 2, :], v_ready)
                if forget:
                    forget_bias_tiles()
                softmax_max(H - 1)
                mix_split_lo(H - 2)
                split((n + 2) * 2 + 1)
                softmax_norm(H - 1)

            split(Count(2 * HEADS))
            split(Count(2 * HEADS + 1))
            split(Count(2 * HEADS + 2))
            out_early(0, Count(KT - 1))
            split(Count(2 * HEADS + 3))
            out_late(0, Count(KT - 1))
            for H in range(4):
                head_slots(Count(H), H == 0)
            with dve.Fori(0, N_HEADS // 2 - 2) as i:
                for g in range(2):
                    head_slots(Count(4 + g, i, 2))
            last_head = N_HEADS - 1
            head_mean_square(Count(last_head))
            norm_k(Count(last_head))
            softmax_max(Count(last_head))
            mix_split_lo(Count(last_head - 1))
            softmax_norm(Count(last_head))
            mix_split_lo(Count(last_head))

            def mixed_slot(n, j):
                b = j + B_W_OUT
                split(n * 2)
                add_halves(b)
                add_to_x(b, j, 1.0)
                split(n * 2 + 1)
                x_split_lo(j + 2 * KT, j)

            for j in range(2):
                mixed_slot(Count(W_OUT + 2 + j), Count(j))
            with dve.Fori(0, (KT - 4) // UNROLL) as i:
                for q in range(UNROLL):
                    mixed_slot(Count(W_OUT + 4 + q, i, UNROLL), Count(2 + q, i, UNROLL))
            for j in range(2):
                mixed_slot(Count(FFN_IN[1] + j), Count(KT - 2 + j))
            swiglu(1)
            out_early(1, Count(KT - 1))


def buckets():
    d = np.arange(SEQ, dtype=np.float32)
    exact = NUM_BUCKETS // 2
    large = exact + (np.log(np.maximum(d, np.float32(1)) / np.float32(exact)) / np.float32(math.log(MAX_DISTANCE / exact))
                     * np.float32(NUM_BUCKETS - exact)).astype(np.int32)
    return np.where(np.arange(SEQ) < exact, np.arange(SEQ), np.minimum(large, NUM_BUCKETS - 1))


def constants():
    dist = np.arange(SEQ)
    count = sum(((dist % d == 0) & (dist <= w)).astype(np.float32) for w, d in PATTERNS)
    one_hot = np.zeros((NUM_BUCKETS, VEC), np.float32)
    vec_mask = np.full((H_A, VEC), MASKED, np.float32)
    for d, bucket in enumerate(buckets()):
        if count[d]:
            one_hot[bucket, SEQ - 1 - d] = 1
            vec_mask[:, SEQ - 1 - d] = 0
    p = np.arange(P)[:, None]
    delta = np.concatenate([p - np.arange(P)[None], P + p - np.arange(SEQ)[None]], axis=1)
    c_mult = np.where(delta >= 0, count[np.maximum(delta, 0)], 0).astype(np.float32)
    c_causal = np.where(delta >= 0, 0, MASKED).astype(np.float32)
    j = np.arange(TB)[None, :, None] * P + np.arange(P)[:, None, None]
    c_upper = (j <= np.arange(SEQ)[None, None, :]).astype(np.float32)
    return {"c_one_hot": one_hot, "c_vec_mask": vec_mask, "c_mult": c_mult, "c_causal": c_causal, "c_upper": c_upper}


def kernel(**inputs):
    import concourse.bacc as bacc
    from concourse.bass_utils import run_bass_kernel_spmd

    nc = bacc.Bacc("TRN2", target_bir_lowering=False, num_devices=1)
    arrays = {name: np.ascontiguousarray(a) for name, a in {**inputs, **constants()}.items()}
    io = {name: nc.dram_tensor(name, a.shape, mybir.dt.from_np(a.dtype), kind="ExternalInput").ap() for name, a in arrays.items()}
    out = nc.dram_tensor("out", (1, SEQ, D_MODEL), mybir.dt.float32, kind="ExternalOutput").ap()
    layer(nc, io, out)
    result = run_bass_kernel_spmd(nc, [arrays], core_ids=[0])
    return result.results[0]["out"]
```

```python
import math
from contextlib import ExitStack

import numpy as np
import concourse.bass as bass
from concourse import mybir

P = 128
D_MODEL, SEQ, HEAD_DIM = 2048, 256, 128
D_FF = ((8 * D_MODEL // 3 + 127) // 128) * 128
KT = D_MODEL // P
FT = D_FF // P
TB = SEQ // P
H_A = H_B = 8
N_HEADS = H_A + H_B
D_A = H_A * HEAD_DIM
EPS = 1e-6
SCALE = HEAD_DIM ** -0.5
MASKED = -1e30
NUM_BUCKETS, MAX_DISTANCE = 32, 2048
PATTERNS = ((128, 1), (512, 4), (2048, 16))
VEC = 384

HALF = KT // 2
OUT_TILES = [min(KT, FT - KT * t) for t in range(3)]
RAW_SLOTS, HALF_SLOTS = 3, 4
UNROLL = 6

FFN_IN = [0, 0]
FFN_OUT = [0, 0]
FFN_OUT[0] = 2 * FT
HEADS = FFN_OUT[0] + 3 * KT
W_OUT = HEADS + 3 * N_HEADS
FFN_IN[1] = W_OUT + KT
FFN_OUT[1] = FFN_IN[1] + 2 * FT
END = FFN_OUT[1] + 3 * KT
B_FFN_IN, B_FFN_OUT = [0, 0], [0, 0]
B_FFN_OUT[0] = 2 * FT
B_HEADS = B_FFN_OUT[0] + KT
B_W_OUT = B_HEADS + 3 * N_HEADS
B_FFN_IN[1] = B_W_OUT + KT
B_FFN_OUT[1] = B_FFN_IN[1] + 2 * FT


class Count:

    def __init__(self, off, reg=None, step=0):
        self.off, self.reg, self.step = off, reg, step

    def __add__(self, k):
        return Count(self.off + k, self.reg, self.step)

    def __sub__(self, k):
        return self + (-k)

    def __mul__(self, k):
        return Count(self.off * k, self.reg, self.step * k)

    def __floordiv__(self, k):
        assert self.step % k == 0
        return Count(self.off // k, self.reg, self.step // k)

    def __mod__(self, k):
        assert self.step % k == 0
        return self.off % k

    def exists(self):
        return self.off >= 0

    def value(self):
        return self.off if self.reg is None or not self.step else self.reg * self.step + self.off


def wait(eng, sem, count):
    if isinstance(count, int):
        count = Count(count)
    assert count.reg is None or count.off >= 0
    if count.reg is None and count.off <= 0:
        return
    eng.wait_ge(sem, count.value())


def cols(index, size):
    return bass.ds((index * size).value(), size)


def layer(nc, io, out):
    f32, f32r = mybir.dt.float32, mybir.dt.float32r
    ALU, ACT, AX = mybir.AluOpType, mybir.ActivationFunctionType, mybir.AxisListType
    ctx = ExitStack()
    with ctx:
        base = -(-nc.sbuf_base // 64) * 64
        place = [base]

        def sb(name, shape, dtype=f32):
            size = -(-int(np.prod(shape[1:])) * 4 // 32) * 32
            t = nc.alloc_sbuf_tensor_at(name, shape, dtype, offset=place[0])
            place[0] += size
            return t

        xT = sb("xT", [P, KT * SEQ])
        xs_at = place[0]
        xs = sb("xs", [P, KT, 2, SEQ], f32r)
        raw = sb("raw", [P, RAW_SLOTS, KT, P])
        whi = sb("whi", [P, HALF_SLOTS, HALF, P], f32r)
        wlo = sb("wlo", [P, HALF_SLOTS, HALF, P], f32r)
        main = sb("main", [P, 2, SEQ])
        total = sb("total", [P, 2, SEQ])
        xsq = sb("xsq", [P, 2, SEQ])
        ssq = sb("ssq", [P, SEQ])
        rstd = sb("rstd", [P, SEQ])
        gate_at = place[0]
        gate, silu, up, act_f = (sb(n, [P, SEQ]) for n in ("gate", "silu", "up", "act_f"))
        ident = sb("ident", [P, P])
        gain_rows = sb("gain_rows", [KT, P])
        gain_rows2 = sb("gain_rows2", [2 * KT + 4, P])
        gains = sb("gains", [P, 64])
        gqk = sb("gqk", [P, 2])
        inv_d = sb("inv_d", [P, 1])
        inv_h = sb("inv_h", [P, 1])
        inv_hr = sb("inv_hr", [P, 1], f32r)
        neg_half = sb("neg_half", [P, TB])
        xss4 = sb("xss4", [P, TB, 4])
        xss = sb("xss", [P, TB])
        xms = sb("xms", [P, TB])
        xrs = sb("xrs", [P, TB])
        f_bias = sb("f_bias", [H_B, 1])
        wf = sb("wf", [P, KT, H_B])
        wf_hi = sb("wf_hi", [P, KT, H_B], f32r)
        wf_lo = sb("wf_lo", [P, KT, H_B], f32r)
        vec = sb("vec", [H_A, VEC])
        arena = place[0]
        act = sb("act", [P, FT, 2, SEQ], f32r)
        ends = [place[0]]
        place[0] = arena
        x_in = sb("x_in", [P, TB, D_MODEL])
        x_in_sq = sb("x_in_sq", [P, 4, TB, D_MODEL // 4])
        table = sb("table", [NUM_BUCKETS, H_A])
        one_hot = sb("one_hot", [NUM_BUCKETS, VEC])
        vec_mask = sb("vec_mask", [H_A, VEC])
        ends.append(place[0])
        place[0] = arena
        mix = sb("mix", [P, N_HEADS, 2, SEQ], f32r)
        dmat = sb("dmat", [P, N_HEADS * 3 * P])
        mult = sb("mult", [P, 3 * P])
        causal = sb("causal", [P, 3 * P])
        upper = sb("upper", [P, TB, SEQ])
        qT = sb("qT", [P, 2, SEQ])
        kT, vT, qn, kn = (sb(n, [P, SEQ]) for n in ("kT", "vT", "qn", "kn"))
        vN = sb("vN", [P, 2, TB, P])
        hsq = xsq
        hsq_hi, hsq_lo = (sb(n, [P, 2, 2 * SEQ], f32r) for n in ("hsq_hi", "hsq_lo"))
        prob, pnorm, probT = (sb(n, [P, 3 * P]) for n in ("prob", "pnorm", "probT"))
        f_main, f_tot, f_exp = (t[0:H_B, :] for t in (gate, silu, up))
        nlfT = sb("nlfT", [P, TB, H_B])
        ncum = sb("ncum", [P, TB, H_B])
        hms, hrs = (sb(n, [P, 2 * SEQ]) for n in ("hms", "hrs"))
        hcorr = nc.alloc_sbuf_tensor_at("hcorr", [P, 2 * SEQ], f32, offset=gate_at)
        mx, nmx, den, rden = (sb(n, [P, TB]) for n in ("mx", "nmx", "den", "rden"))
        ends.append(place[0])
        assert max(ends) <= nc.sbuf_usable_end, (ends, nc.sbuf_usable_end)
        place[0] = xs_at
        x_final = sb("x_final", [P, 2, SEQ])
        ost = sb("ost", [P, 2, TB, P])

        def ps(name):
            return ctx.enter_context(nc.psum_tensor(name, [P, 512], f32))

        acc = [ps("acc0"), ps("acc1")]
        ps_st, ps_bc, ps_v, ps_l, ps_pt, ps_o = (ps(n) for n in ("ps_st", "ps_bc", "ps_v", "ps_l", "ps_pt", "ps_o"))
        x_banks = [ps_bc, ps_v, ps_l, ps_pt]
        row_banks = [ps_pt, ps_o]
        o_banks = [ps_v, ps_l]
        scratch = nc.dram_tensor("bias_vectors", (H_A, P, VEC), f32).ap()

        def sem(name):
            return ctx.enter_context(nc.semaphore(name))

        raw_full = [sem(f"raw_full{s}") for s in range(RAW_SLOTS)]
        weights_hi, weights_lo, weights_used = sem("weights_hi"), sem("weights_lo"), sem("weights_used")
        main_copied, block_summed = sem("main_copied"), sem("block_summed")
        gate_scaled, silu_done, up_scaled, act_done, act_hi, act_ready = (
            sem(n) for n in ("gate_scaled", "silu_done", "up_scaled", "act_done", "act_hi", "act_ready"))
        x_updated, x_hi, x_ready, x_squared, ssq_added = (
            sem(n) for n in ("x_updated", "x_hi", "x_ready", "x_squared", "ssq_added"))
        xms_psum, xms_ready, xrs_ready, rstd_psum, rstd_ready = (
            sem(n) for n in ("xms_psum", "xms_ready", "xrs_ready", "rstd_psum", "rstd_ready"))
        x_loaded = [sem(f"x_loaded{c}") for c in range(4)]
        ident_zero, ident_ready, small_set, gains_loaded, gains2_loaded, gains_psum, gains_ready, gqk_ready, xss_ready = (
            sem(n) for n in ("ident_zero", "ident_ready", "small_set", "gains_loaded", "gains2_loaded", "gains_psum",
                             "gains_ready", "gqk_ready", "xss_ready"))
        xss4_ready, table_warm = sem("xss4_ready"), sem("table_warm")
        f_loaded, wf_hi_ready, wf_ready = sem("f_loaded"), sem("wf_hi_ready"), sem("wf_ready")
        x_psum = sem("x_psum")
        vec_loaded, vec_psum, vec_ready, vec_stored = (
            sem(n) for n in ("vec_loaded", "vec_psum", "vec_ready", "vec_stored"))
        mixer_loaded = sem("mixer_loaded")
        f_psum, f_copied, f_step, f_exped, nlf_ready, nlfT_psum, nlfT_ready, ncum_psum, ncum_ready, row_psum, d_built = (
            sem(n) for n in ("f_psum", "f_copied", "f_step", "f_exped", "nlf_ready", "nlfT_psum", "nlfT_ready",
                             "ncum_psum", "ncum_ready", "row_psum", "d_built"))
        q_ready, k_ready, v_ready, inv_hr_ready = (
            sem(n) for n in ("q_ready", "k_ready", "v_ready", "inv_hr_ready"))
        squared, squared_hi, squared_ready = (sem(n) for n in ("squared", "squared_hi", "squared_ready"))
        hms_psum, hms_ready, hlog_ready, hrs_guessed, hcorr_step, hrs_ready, qn_ready, kn_ready = (
            sem(n) for n in ("hms_psum", "hms_ready", "hlog_ready", "hrs_guessed", "hcorr_step", "hrs_ready", "qn_ready", "kn_ready"))
        vN_psum, vN_ready, logit_psum, logit_ready, max_ready, nmax_ready, exp_ready = (
            sem(n) for n in ("vN_psum", "vN_ready", "logit_psum", "logit_ready", "max_ready", "nmax_ready", "exp_ready"))
        den_ready, rden_ready, prob_ready, probT_psum, probT_ready, o_psum, mix_hi, mix_ready = (
            sem(n) for n in ("den_ready", "rden_ready", "prob_ready", "probT_psum", "probT_ready", "o_psum", "mix_hi", "mix_ready"))
        ost_psum, ost_ready = sem("ost_psum"), sem("ost_ready")
        stored = [sem("stored0"), sem("stored1")]

        def x_tile(j):
            return xT[:, cols(j, SEQ)]

        def x_split(j, part):
            return xs[:, bass.ds(j.value(), 1), part, :].rearrange("p a s -> p (a s)")

        def d_tile(head, lo, hi):
            at = (head // 2 + (H_A if head % 2 else 0)) * (3 * P)
            return dmat[:, bass.ds((at + lo).value(), hi - lo)]

        def mix_tile(head, part):
            at = head // 2 + (H_A if head % 2 else 0)
            return mix[:, bass.ds(at.value(), 1), part, :].rearrange("p a s -> p (a s)")

        def half_tiles(h_in_block):
            t, half = h_in_block // 2, h_in_block % 2
            return min(HALF, OUT_TILES[t] - HALF * half)

        block = ctx.enter_context(nc.Block())

        @block.sync
        def _(sp):
            def piece(n, src, tiles=KT):
                wait(sp, weights_lo, (n - RAW_SLOTS + 1) * 2)
                sp.dma_start(raw[:, n % RAW_SLOTS, 0:tiles, :], src).then_inc(raw_full[n % RAW_SLOTS], 16)

            sp.dma_start(gain_rows[:], io["ffn1_norm"][0].rearrange("(k p) -> k p", p=P)).then_inc(gains_loaded, 16)
            x_rows = io["x"][0].rearrange("(b p) d -> p b d", p=P)

            def x_quarters(quarters):
                w = D_MODEL // 4
                for c in quarters:
                    sp.dma_start(x_in[:, :, c * w:(c + 1) * w], x_rows[:, :, c * w:(c + 1) * w]).then_inc(x_loaded[c], 16)

            x_quarters((0, 1))
            for u in range(2):
                w_in = io[f"ffn{u + 1}_w_in"][0].rearrange("(k p) f -> p k f", p=P)
                w_out = io[f"ffn{u + 1}_w_out"][0].rearrange("(t p) d -> p t d", p=P)

                def in_piece(q, n):
                    c = (q // 2) * P + (D_FF if q % 2 else 0)
                    piece(n, w_in[:, :, bass.ds(c.value(), P)])

                in_piece(Count(0), Count(FFN_IN[u]))
                if u == 0:
                    x_quarters((2, 3))
                in_piece(Count(1), Count(FFN_IN[u] + 1))
                with sp.Fori(0, (2 * FT - 2) // UNROLL) as i:
                    for q in range(2, 2 + UNROLL):
                        in_piece(Count(q, i, UNROLL), Count(FFN_IN[u] + q, i, UNROLL))
                with sp.Fori(0, KT // 2) as i:
                    for q in range(UNROLL):
                        j, t = Count(q // 3, i, 2), q % 3
                        piece(Count(FFN_OUT[u] + q, i, UNROLL),
                              w_out[:, KT * t:KT * t + OUT_TILES[t], cols(j, P)], OUT_TILES[t])
                if u == 0:
                    w_mix = io["w_in"][0].rearrange("(k p) f -> p k f", p=P)
                    with sp.Fori(0, N_HEADS // 2) as i:
                        for q in range(UNROLL):
                            c = Count((q // 3) * 3 * D_A + (q % 3) * D_A, i, HEAD_DIM)
                            piece(Count(HEADS + q, i, UNROLL), w_mix[:, :, bass.ds(c.value(), P)])
                    w_o = io["w_out"][0].rearrange("(k p) d -> p k d", p=P)
                    for j in range(4):
                        piece(Count(W_OUT + j), w_o[:, :, j * P:(j + 1) * P])
                    with sp.Fori(0, (KT - 4) // UNROLL) as i:
                        for q in range(UNROLL):
                            piece(Count(W_OUT + 4 + q, i, UNROLL), w_o[:, :, cols(Count(4 + q, i, UNROLL), P)])

        @block.gpsimd
        def _(pool):
            pool.memset(inv_d[:], 1.0 / D_MODEL).then_inc(small_set, 1)
            pool.memset(inv_h[:], 1.0 / HEAD_DIM).then_inc(small_set, 1)
            pool.memset(neg_half[:], -0.5).then_inc(small_set, 1)
            pool.memset(ident[:], 0.0).then_inc(ident_zero, 1)
            pool.wait_ge(ident_zero, 1)
            pool.affine_select(out=ident[:], in_=ident[:], compare_op=ALU.not_equal, fill=1.0, base=0,
                               pattern=[[-1, P]], channel_multiplier=1).then_inc(ident_ready, 1)
            pool.dma_start(table[:], io["rel_bias_table"]).then_inc(vec_loaded, 16)
            pool.dma_start(one_hot[:], io["c_one_hot"]).then_inc(vec_loaded, 16)
            pool.dma_start(vec_mask[:], io["c_vec_mask"]).then_inc(vec_loaded, 16)
            for s, name in enumerate(("mix_norm", "ffn2_norm")):
                pool.dma_start(gain_rows2[s * KT:(s + 1) * KT, :], io[name][0].rearrange("(k p) -> k p", p=P)).then_inc(gains2_loaded, 16)
            for s, name in enumerate(("q_norm_a", "k_norm_a", "q_norm_b", "k_norm_b")):
                pool.dma_start(gain_rows2[2 * KT + s:2 * KT + s + 1, :], io[name]).then_inc(gains2_loaded, 16)
            pool.dma_start(wf[:], io["w_in"][0].rearrange("(k p) f -> p k f", p=P)[:, :, 6 * D_A:6 * D_A + H_B]).then_inc(f_loaded, 16)
            pool.dma_start(f_bias[:], io["forget_bias"].rearrange("a h -> h a")).then_inc(f_loaded, 16)

            def add_square(X, j0):
                wait(pool, x_squared, X + 1)
                if j0:
                    wait(pool, xms_psum, X.off // KT)
                    pool.tensor_copy(ssq[:], xsq[:, X % 2, :]).then_inc(ssq_added, 1)
                else:
                    wait(pool, ssq_added, X)
                    pool.tensor_tensor(ssq[:], ssq[:], xsq[:, X % 2, :], ALU.add).then_inc(ssq_added, 1)

            def x_power(s):
                wait(pool, xms_ready, s + 1)
                pool.tensor_tensor(xrs[:], xms[:], neg_half[:], ALU.pow).then_inc(xrs_ready, 1)

            pool.wait_ge(small_set, 3)
            x_power(0)
            pool.wait_ge(vec_ready, 1)
            pool.dma_start(scratch, vec[:].rearrange("h (a v) -> h a v", a=1).to_broadcast([H_A, P, VEC])).then_inc(vec_stored, 16)
            for s in (1, 2):
                first = KT * (s - 1)
                add_square(Count(first), True)
                add_square(Count(first + 1), False)
                with pool.Fori(0, KT // 2 - 1) as i:
                    for j in range(2):
                        add_square(Count(first + 2 + j, i, 2), False)
                if s == 1:
                    pool.wait_ge(weights_used, 2 * HEADS)
                    pool.wait_ge(vec_stored, 16)
                    pool.dma_start(mult[:], io["c_mult"]).then_inc(mixer_loaded, 16)
                    pool.dma_start(causal[:], io["c_causal"]).then_inc(mixer_loaded, 16)
                    pool.dma_start(upper[:], io["c_upper"]).then_inc(mixer_loaded, 16)
                    d_a = dmat[:, 0:H_A * 3 * P].rearrange("p (h c) -> p h c", h=H_A)
                    for b in range(TB):
                        src = bass.AP(tensor=scratch.tensor, offset=SEQ - 1 - b * P,
                                      ap=[[VEC - 1, P], [P * VEC, H_A], [1, (b + 1) * P]])
                        pool.dma_start(d_a[:, :, b * P:b * P + (b + 1) * P], src).then_inc(mixer_loaded, 16)
                x_power(s)

        @block.tensor
        def _(pe):
            mm = nc.tensor.matmul

            def pair(bank, slot, kk, moving, first, last, m=P):
                mm(bank[:, 0:2 * SEQ], whi[:, slot, kk, :], moving.rearrange("p a s -> p (a s)"), start=first, stop=False,
                   skip_group_check=True)
                return mm(bank[:, SEQ:2 * SEQ], wlo[:, slot, kk, :], moving[:, 0, :], start=False, stop=last,
                          skip_group_check=True)

            def half(h, bank, tiles, k0, k_total, moving, before=None):
                wait(pe, weights_lo, h + 1)
                for kk in range(tiles):
                    k = k0 + kk
                    if before:
                        before(k)
                    last = pair(bank, h % HALF_SLOTS, kk, moving[:, k, :, :], k == 0, k == k_total - 1)
                last.then_inc(weights_used, 1)

            def in_block(n, b, moving, before=None, between=None):
                wait(pe, block_summed, b - 1)
                half(n * 2, acc[b % 2], HALF, 0, KT, moving, before)
                if between:
                    between()
                half(n * 2 + 1, acc[b % 2], HALF, HALF, KT, moving, before)

            def out_block(n, b, before=None):
                wait(pe, block_summed, b - 1)
                for h in range(6):
                    half(n * 2 + h, acc[b % 2], half_tiles(h), HALF * h, FT, act, before)

            def x_stats(s):
                wait(pe, ssq_added, KT * s)
                for b in range(TB):
                    last = mm(ps_st[:, b:b + 1], ssq[:, b * P:(b + 1) * P], inv_d[:], start=True, stop=True)
                last.then_inc(xms_psum, 1)

            def x_spread(s):
                wait(pe, xrs_ready, s + 1)
                for b in range(TB):
                    last = mm(ps_bc[:, b * P:(b + 1) * P], xrs[:, b:b + 1].to_broadcast([P, P]), ident[:],
                              start=True, stop=True, skip_group_check=True)
                last.then_inc(rstd_psum, 1)

            pe.wait_ge(gains_loaded, 16)
            pe.wait_ge(ident_ready, 1)
            nc.tensor.transpose(ps_st[:, 0:KT], gain_rows[:], ident[0:KT, 0:KT]).then_inc(gains_psum, 1)

            def x_turn(j):
                if j % 4 == 0:
                    pe.wait_ge(x_loaded[j // 4], 16)
                wait(pe, x_updated, j - 3)
                for b in range(TB):
                    last = nc.tensor.transpose(x_banks[j % 4][:, b * P:(b + 1) * P], x_in[:, b, j * P:(j + 1) * P], ident[:])
                last.then_inc(x_psum, 1)

            turned = HALF + 2
            for j in range(turned):
                x_turn(j)

            def first_tile_ready(k):
                if k + turned < KT:
                    x_turn(k + turned)
                wait(pe, x_ready, k + 1)

            def small_products():
                pe.wait_ge(gains2_loaded, 6 * 16)
                pe.wait_ge(gains_ready, 1)
                rows = 2 * KT + 4
                nc.tensor.transpose(ps_st[:, 0:rows], gain_rows2[:], ident[0:rows, 0:rows]).then_inc(gains_psum, 1)
                pe.wait_ge(vec_loaded, 48)
                mm(ps_o[0:H_A, 0:VEC], table[:], one_hot[:], start=True, stop=True).then_inc(vec_psum, 1)

            spread_tile = (4, 6)

            def ffn_in(u, before, s):
                n, b = FFN_IN[u], B_FFN_IN[u]
                in_block(Count(n), Count(b), xs, before)
                if u:
                    x_stats(s)
                else:
                    small_products()

                def spread_at(k):
                    if k == spread_tile[u]:
                        x_spread(s)

                in_block(Count(n + 1), Count(b + 1), xs, spread_at)
                with pe.Fori(0, (2 * FT - 2) // UNROLL) as i:
                    for q in range(2, 2 + UNROLL):
                        in_block(Count(n + q, i, UNROLL), Count(b + q, i, UNROLL), xs)

            def tile_ready(first):
                return lambda k: wait(pe, x_ready, first + k + 1)

            ffn_in(0, first_tile_ready, 0)
            out_block(Count(FFN_OUT[0]), Count(B_FFN_OUT[0]), lambda k: wait(pe, act_ready, k + 1))
            out_block(Count(FFN_OUT[0] + 3), Count(B_FFN_OUT[0] + 1))
            with pe.Fori(0, KT // 2 - 1) as i:
                for j in range(2):
                    out_block(Count(FFN_OUT[0] + 6 + 3 * j, i, 6), Count(B_FFN_OUT[0] + 2 + j, i, 2))

            def head_stats(H):
                if not H.exists():
                    return
                wait(pe, squared_ready, H * 2 + 2)
                mm(ps_st[:], inv_hr[:].to_broadcast([P, P]), hsq_hi[:, H % 2, :], start=True, stop=False)
                mm(ps_st[:], inv_hr[:].to_broadcast([P, P]), hsq_lo[:, H % 2, :], start=False, stop=True).then_inc(hms_psum, 1)

            def v_turn(H):
                if not H.exists():
                    return
                wait(pe, v_ready, H + 1)
                wait(pe, vN_ready, H)
                for b in range(TB):
                    last = nc.tensor.transpose(ps_v[:, b * P:(b + 1) * P], vT[:, b * P:(b + 1) * P], ident[:])
                last.then_inc(vN_psum, 1)

            def logits(H):
                if not H.exists():
                    return
                wait(pe, qn_ready, H + 1)
                wait(pe, kn_ready, H + 1)
                mm(ps_l[:, 0:P], qn[:, 0:P], kn[:, 0:P], start=True, stop=True, skip_group_check=True)
                mm(ps_l[:, P:3 * P], qn[:, P:2 * P], kn[:], start=True, stop=True,
                   skip_group_check=True).then_inc(logit_psum, 1)

            def prob_turn(H):
                if not H.exists():
                    return
                wait(pe, prob_ready, H + 1)
                for c in range(3):
                    last = nc.tensor.transpose(ps_pt[:, c * P:(c + 1) * P], pnorm[:, c * P:(c + 1) * P], ident[:])
                last.then_inc(probT_psum, 1)

            def weighted(H):
                if not H.exists():
                    return
                wait(pe, probT_ready, H + 1)
                wait(pe, vN_ready, H + 1)
                wait(pe, mix_ready, H)
                mm(ps_o[:, 0:SEQ], vN[:, H % 2, 0, :], probT[:, 0:SEQ], start=True, stop=False, skip_group_check=True)
                mm(ps_o[:, P:SEQ], vN[:, H % 2, 1, :], probT[:, SEQ:3 * P], start=False, stop=True,
                   skip_group_check=True).then_inc(o_psum, 1)

            def forget_product():
                pe.wait_ge(wf_ready, 1)
                for k in range(KT):
                    mm(ps_l[0:H_B, 0:2 * SEQ], wf_hi[:, k, :], xs[:, k, :, :].rearrange("p a s -> p (a s)"),
                       start=k == 0, stop=False, skip_group_check=True)
                    last = mm(ps_l[0:H_B, SEQ:2 * SEQ], wf_lo[:, k, :], xs[:, k, 0, :], start=False, stop=k == KT - 1,
                              skip_group_check=True)
                last.then_inc(f_psum, 1)

            def forget_turn():
                pe.wait_ge(nlf_ready, 1)
                for b in range(TB):
                    last = nc.tensor.transpose(ps_v[:, b * H_B:(b + 1) * H_B], f_tot[:, b * P:(b + 1) * P], ident[0:H_B, 0:H_B])
                last.then_inc(nlfT_psum, 1)

            def forget_sums():
                pe.wait_ge(nlfT_ready, 1)
                pe.wait_ge(mixer_loaded, 5 * 16)
                mm(ps_st[:, 0:H_B], upper[:, 0, 0:P], nlfT[:, 0, :], start=True, stop=True, skip_group_check=True)
                mm(ps_st[:, H_B:2 * H_B], upper[:, 0, P:SEQ], nlfT[:, 0, :], start=True, stop=False, skip_group_check=True)
                mm(ps_st[:, H_B:2 * H_B], upper[:, 1, P:SEQ], nlfT[:, 1, :], start=False, stop=True,
                   skip_group_check=True).then_inc(ncum_psum, 1)
                for h in range(H_B):
                    bank = row_banks[h % 2]
                    wait(pe, d_built, h - 1)
                    mm(bank[:, 0:SEQ], nlfT[:, 0, h:h + 1].to_broadcast([P, P]), upper[:, 0, :], start=True, stop=False,
                       skip_group_check=True)
                    mm(bank[:, P:SEQ], nlfT[:, 1, h:h + 1].to_broadcast([P, P]), upper[:, 1, P:SEQ], start=False, stop=True,
                       skip_group_check=True).then_inc(row_psum, 1)

            def head(n, b, H, before=None, forget=False):
                def stats_at(k):
                    if before:
                        before(k)
                    if k == 2:
                        head_stats(H - 1)

                in_block(n, b, xs, stats_at)
                if forget:
                    x_stats(1)
                    forget_product()
                    x_spread(1)
                in_block(n + 1, b + 1, xs)
                if forget:
                    forget_turn()
                v_turn(H - 1)
                prob_turn(H - 2)
                in_block(n + 2, b + 2, xs)
                if forget:
                    forget_sums()
                logits(H - 1)
                weighted(H - 2)

            for H in range(4):
                head(Count(HEADS + 3 * H), Count(B_HEADS + 3 * H), Count(H), tile_ready(KT) if H == 0 else None, H == 0)
            with pe.Fori(0, N_HEADS // 2 - 2) as i:
                for g in range(2):
                    head(Count(HEADS + 12 + 3 * g, i, 6), Count(B_HEADS + 12 + 3 * g, i, 6), Count(4 + g, i, 2))

            last_head = N_HEADS - 1

            def part(j, tiles, first=False, used=0):
                h0 = 2 * (W_OUT + j)
                for k in tiles:
                    if first and k == tiles[0]:
                        wait(pe, block_summed, B_W_OUT + j - 1)
                        wait(pe, weights_lo, h0 + 2)
                    done = pair(acc[(B_W_OUT + j) % 2], (h0 + k // HALF) % HALF_SLOTS, k % HALF, mix[:, k, :, :],
                                first and k == tiles[0], k == KT - 1)
                if used:
                    done.then_inc(weights_used, used)

            pe.wait_ge(mix_ready, last_head - 3)
            part(0, [0, 1], True)
            head_stats(Count(last_head))
            part(0, [2, 3, 4, 5, 8, 9, 10, 11, 12, 13])
            v_turn(Count(last_head))
            pe.wait_ge(mix_ready, last_head - 1)
            part(0, [6, 14])
            part(1, [0, 1, 2, 3, 4, 5, 6], True)
            prob_turn(Count(last_head - 1))
            part(1, [8, 9])
            weighted(Count(last_head - 1))
            logits(Count(last_head))
            part(1, [10, 11, 12, 13, 14])
            pe.wait_ge(mix_ready, last_head)
            part(0, [7], used=1)
            part(1, [7])
            prob_turn(Count(last_head))
            weighted(Count(last_head))
            pe.wait_ge(mix_ready, last_head + 1)
            part(0, [15], used=2)
            part(1, [15], used=1)
            for j in range(2, 4):
                in_block(Count(W_OUT + j), Count(B_W_OUT + j), mix)
            with pe.Fori(0, (KT - 4) // UNROLL) as i:
                for q in range(4, 4 + UNROLL):
                    in_block(Count(W_OUT + q, i, UNROLL), Count(B_W_OUT + q, i, UNROLL), mix)

            def out_turn(j):
                wait(pe, x_updated, j + 3 * KT + 1)
                wait(pe, ost_ready, j - 1)
                for b in range(TB):
                    last = nc.tensor.transpose(o_banks[j % 2][:, b * P:(b + 1) * P],
                                               x_final[:, j % 2, b * P:(b + 1) * P], ident[:])
                last.then_inc(ost_psum, 1)

            ffn_in(1, tile_ready(2 * KT), 2)
            out_block(Count(FFN_OUT[1]), Count(B_FFN_OUT[1]), lambda k: wait(pe, act_ready, FT + k + 1))
            out_block(Count(FFN_OUT[1] + 3), Count(B_FFN_OUT[1] + 1))
            out_turn(Count(0))
            with pe.Fori(0, KT // 2 - 1) as i:
                for j in range(2):
                    out_block(Count(FFN_OUT[1] + 6 + 3 * j, i, 6), Count(B_FFN_OUT[1] + 2 + j, i, 2))
                    out_turn(Count(1 + j, i, 2))
            out_turn(Count(KT - 1))

        @block.scalar
        def _(act_e):
            A = nc.scalar.activation

            def split(h, tiles=HALF):
                n = h // 2
                slot, first = n % RAW_SLOTS, HALF * (h % 2)
                wait(act_e, raw_full[slot], (n // RAW_SLOTS + 1) * 16)
                wait(act_e, weights_used, h - HALF_SLOTS + 1)
                A(whi[:, h % HALF_SLOTS, 0:tiles, :], raw[:, slot, first:first + tiles, :], ACT.Copy).then_inc(weights_hi, 1)

            def copy_main(b, used):
                wait(act_e, weights_used, used)
                A(main[:, b % 2, :], acc[b % 2][:, 0:SEQ], ACT.Copy).then_inc(main_copied, 1)

            def x_split_hi(X, j):
                wait(act_e, x_updated, X + 1)
                A(x_split(j, 0), x_tile(j), ACT.Copy, scale=gains[:, bass.ds(X.value(), 1)]).then_inc(x_hi, 1)

            def x_square_free(X):
                wait(act_e, ssq_added, X - (KT + 1))

            def x_square(X, j):
                A(xsq[:, X % 2, :], x_tile(j), ACT.Square).then_inc(x_squared, 1)

            def copy_rstd(s):
                wait(act_e, rstd_psum, s + 1)
                A(rstd[:], ps_bc[:, 0:SEQ], ACT.Copy).then_inc(rstd_ready, 1)

            act_e.wait_ge(small_set, 2)
            A(xss4[:, 0, 0:1], inv_h[:], ACT.Square).then_inc(table_warm, 1)
            act_e.wait_ge(table_warm, 1)
            act_e.wait_ge(gains_ready, 1)
            for j in range(KT):
                x_split_hi(Count(j), Count(j))
                if j in (6, 11, KT - 1):
                    split(Count(j // 5 - 1))
                if j % 2:
                    c, b = j // 2 // TB, j // 2 % TB
                    w = D_MODEL // 4
                    act_e.wait_ge(x_loaded[c], 16)
                    A(x_in_sq[:, c, b, :], x_in[:, b, c * w:(c + 1) * w], ACT.Square, accum_out=xss4[:, b, c:c + 1]).then_inc(xss4_ready, 1)
            split(Count(3))
            act_e.wait_ge(f_loaded, 32)
            A(wf_hi[:], wf[:], ACT.Copy).then_inc(wf_hi_ready, 1)
            A(inv_hr[:], inv_h[:], ACT.Copy).then_inc(inv_hr_ready, 1)

            def hidden_early(u, p):
                copy_main(p + B_FFN_IN[u], (p + FFN_IN[u] + 1) * 2)

            def hidden_late(u, p, is_up):
                F = p // 2 + u * FT
                if is_up:
                    wait(act_e, act_done, F + 1)
                    A(act[:, bass.ds((p // 2).value(), 1), 0, :].rearrange("p a s -> p (a s)"), act_f[:], ACT.Copy).then_inc(act_hi, 1)
                else:
                    wait(act_e, gate_scaled, F + 1)
                    A(silu[:], gate[:], ACT.Silu).then_inc(silu_done, 1)

            def out_late(u, j):
                if u == 0:
                    x_square_free(j + KT)
                    x_split_hi(j + KT, j)
                    x_square(j + KT, j)
                else:
                    store(j - 1)

            def store(j):
                if not j.exists():
                    return
                wait(act_e, ost_psum, j + 1)
                wait(act_e, stored[j % 2], (j // 2) * 16)
                A(ost[:, j % 2, :, :], o_banks[j % 2][:, 0:SEQ].rearrange("p (b d) -> p b d", b=TB), ACT.Copy).then_inc(ost_ready, 1)
                wait(act_e, ost_ready, j + 1)
                act_e.dma_start(out[0].rearrange("(b p) d -> p b d", p=P)[:, :, cols(j, P)], ost[:, j % 2, :, :]).then_inc(stored[j % 2], 16)

            def swiglu(u):
                copy_rstd(2 * u)
                with act_e.Fori(0, (2 * FT - 2) // UNROLL) as i:
                    for q in range(2, 2 + UNROLL):
                        n, p = Count(FFN_IN[u] + q, i, UNROLL), Count(q - 2, i, UNROLL)
                        split(n * 2)
                        hidden_early(u, p)
                        split(n * 2 + 1)
                        hidden_late(u, p, q % 2)
                for q in range(UNROLL):
                    n = Count(FFN_OUT[u] + q)
                    split(n * 2, half_tiles(q % 3 * 2))
                    if q < 2:
                        hidden_early(u, Count(2 * FT - 2 + q))
                    if q == 4:
                        copy_main(Count(B_FFN_OUT[u]), Count(FFN_OUT[u] + 3) * 2)
                    split(n * 2 + 1, half_tiles(q % 3 * 2 + 1))
                    if q < 2:
                        hidden_late(u, Count(2 * FT - 2 + q), q)
                    if q == 4:
                        out_late(u, Count(0))
                with act_e.Fori(0, KT // 2 - 1) as i:
                    for q in range(UNROLL, 2 * UNROLL):
                        n = Count(FFN_OUT[u] + q, i, UNROLL)
                        j = Count((q - 4) // 3, i, 2)
                        split(n * 2, half_tiles(q % 3 * 2))
                        if q % 3 == 1:
                            copy_main(j + B_FFN_OUT[u], (j * 3 + (FFN_OUT[u] + 3)) * 2)
                        split(n * 2 + 1, half_tiles(q % 3 * 2 + 1))
                        if q % 3 == 1:
                            out_late(u, j)

            def last_out(u):
                copy_main(Count(B_FFN_OUT[u] + KT - 1), Count(FFN_OUT[u] + 3 * KT) * 2)

            swiglu(0)

            def exps(H):
                if not H.exists():
                    return
                wait(act_e, nmax_ready, H + 1)
                for b in range(TB):
                    c = slice(b * P, b * P + (b + 1) * P)
                    last = A(prob[:, c], prob[:, c], ACT.Exp, bias=nmx[:, b:b + 1],
                             **({"accum_out": den[:, b:b + 1]} if H % 2 else {}))
                last.then_inc(exp_ready, 1)

            def copy_vN(H):
                if H.exists():
                    wait(act_e, vN_psum, H + 1)
                    A(vN[:, H % 2, :, :], ps_v[:, 0:SEQ].rearrange("p (b d) -> p b d", b=TB), ACT.Copy).then_inc(vN_ready, 1)

            def copy_probT(H):
                if H.exists():
                    wait(act_e, probT_psum, H + 1)
                    A(probT[:], ps_pt[:, 0:3 * P], ACT.Copy).then_inc(probT_ready, 1)

            def mix_split_hi(H):
                if H.exists():
                    wait(act_e, o_psum, H + 1)
                    A(mix_tile(H, 0), ps_o[:, 0:SEQ], ACT.Copy).then_inc(mix_hi, 1)

            def head_rstd(H):
                if H.exists():
                    wait(act_e, hms_ready, H + 1)
                    A(hrs[:], hms[:], ACT.Ln, scale=-2.0).then_inc(hlog_ready, 1)
                    wait(act_e, hlog_ready, H + 1)
                    A(hrs[:], hrs[:], ACT.Exp, scale=-0.5).then_inc(hrs_guessed, 1)

            def square_hi(H, c):
                wait(act_e, squared, H * 2 + (c + 1))
                A(hsq_hi[:, H % 2, c * SEQ:(c + 1) * SEQ], hsq[:, c, :], ACT.Copy).then_inc(squared_hi, 1)

            def head_slots(H, forget=False):
                n, b = H * 3 + (HEADS + 2), H * 3 + B_HEADS
                used = H * 6 + 2 * (HEADS + 1)
                split(n * 2)
                copy_main(b, used)
                if forget:
                    wait(act_e, f_psum, 1)
                    A(f_main, ps_l[0:H_B, 0:SEQ], ACT.Copy).then_inc(f_copied, 1)
                    copy_rstd(1)
                head_rstd(H - 1)
                split(n * 2 + 1)
                square_hi(H, 0)
                if forget:
                    wait(act_e, f_step, 4)
                    A(f_exp, f_main, ACT.Exp).then_inc(f_exped, 1)
                    wait(act_e, f_exped, 1)
                    A(f_exp, f_exp, ACT.Ln, bias=1.0).then_inc(f_exped, 1)

                split((n + 1) * 2)
                copy_main(b + 1, used + 2)
                if forget:
                    wait(act_e, nlfT_psum, 1)
                    A(nlfT[:], ps_v[:, 0:TB * H_B].rearrange("p (b h) -> p b h", b=TB), ACT.Copy).then_inc(nlfT_ready, 1)
                copy_vN(H - 1)
                copy_probT(H - 2)
                split((n + 1) * 2 + 1)
                square_hi(H, 1)

                split((n + 2) * 2)
                copy_main(b + 2, used + 4)
                mix_split_hi(H - 2)
                split((n + 2) * 2 + 1)
                exps(H - 1)

            split(Count(2 * HEADS))
            split(Count(2 * HEADS + 1))
            split(Count(2 * HEADS + 2))
            last_out(0)
            split(Count(2 * HEADS + 3))
            out_late(0, Count(KT - 1))
            for H in range(4):
                head_slots(Count(H), H == 0)
            with act_e.Fori(0, N_HEADS // 2 - 2) as i:
                for g in range(2):
                    head_slots(Count(4 + g, i, 2))
            last_head = N_HEADS - 1
            head_rstd(Count(last_head))
            copy_vN(Count(last_head))
            copy_probT(Count(last_head - 1))
            mix_split_hi(Count(last_head - 1))
            exps(Count(last_head))
            copy_probT(Count(last_head))
            mix_split_hi(Count(last_head))

            def mixed_slot(n, j):
                split(n * 2)
                copy_main(j + B_W_OUT, (j + (W_OUT + 1)) * 2)
                split(n * 2 + 1)
                x_square_free(j + 2 * KT)
                x_split_hi(j + 2 * KT, j)
                x_square(j + 2 * KT, j)

            for j in range(2):
                mixed_slot(Count(W_OUT + 2 + j), Count(j))
            with act_e.Fori(0, (KT - 4) // UNROLL) as i:
                for q in range(UNROLL):
                    mixed_slot(Count(W_OUT + 4 + q, i, UNROLL), Count(2 + q, i, UNROLL))
            for j in range(2):
                mixed_slot(Count(FFN_IN[1] + j), Count(KT - 2 + j))
            swiglu(1)
            last_out(1)
            store(Count(KT - 2))
            store(Count(KT - 1))
            for s in range(2):
                act_e.wait_ge(stored[s], 16 * KT // 2)

        @block.vector
        def _(dve):
            V = nc.vector

            def split(h, tiles=HALF):
                n = h // 2
                slot, first = n % RAW_SLOTS, HALF * (h % 2)
                wait(dve, weights_hi, h + 1)
                V.tensor_tensor(wlo[:, h % HALF_SLOTS, 0:tiles, :], raw[:, slot, first:first + tiles, :],
                                whi[:, h % HALF_SLOTS, 0:tiles, :].bitcast(f32), ALU.subtract).then_inc(weights_lo, 1)

            def add_halves(b):
                wait(dve, main_copied, b + 1)
                V.tensor_tensor(total[:, b % 2, :], main[:, b % 2, :], acc[b % 2][:, SEQ:2 * SEQ], ALU.add).then_inc(block_summed, 1)

            def scaled(b, dest, done):
                wait(dve, block_summed, b + 1)
                V.tensor_tensor(dest, total[:, b % 2, :], rstd[:], ALU.mult).then_inc(done, 1)

            def x_split_lo(X, j):
                wait(dve, x_hi, X + 1)
                wait(dve, x_updated, X + 1)
                V.scalar_tensor_tensor(x_split(j, 1), x_tile(j), gains[:, bass.ds(X.value(), 1)],
                                       x_split(j, 0).bitcast(f32), ALU.mult, ALU.subtract).then_inc(x_ready, 1)

            def x_mean_square(s):
                wait(dve, xms_psum, s)
                V.tensor_scalar(xms[:], ps_st[:, 0:TB], EPS, None, ALU.add).then_inc(xms_ready, 1)

            dve.wait_ge(gains_psum, 1)
            V.tensor_copy(gains[:, 0:KT], ps_st[:, 0:KT]).then_inc(gains_ready, 1)
            dve.wait_ge(gains_ready, 1)

            for j in range(KT + 1):
                if j < KT:
                    dve.wait_ge(x_psum, j + 1)
                    V.tensor_copy(x_tile(Count(j)), x_banks[j % 4][:, 0:SEQ]).then_inc(x_updated, 1)
                if j > 0:
                    x_split_lo(Count(j - 1), Count(j - 1))
                if j in (7, 12):
                    split(Count(j // 8))
            split(Count(2))
            dve.wait_ge(xss4_ready, 8)
            V.reduce_sum(xss[:], xss4[:], AX.X).then_inc(xss_ready, 1)
            dve.wait_ge(xss_ready, 1)
            V.tensor_scalar(xms[:], xss[:], 1.0 / D_MODEL, EPS, ALU.mult, ALU.add).then_inc(xms_ready, 1)
            split(Count(3))
            dve.wait_ge(gains_psum, 2)
            V.tensor_copy(gains[:, KT:3 * KT + 4], ps_st[:, 0:2 * KT + 4]).then_inc(gains_ready, 1)
            dve.wait_ge(gains_ready, 2)
            for g in range(2):
                q = 3 * KT + 2 * g
                V.scalar_tensor_tensor(gqk[:, g:g + 1], gains[:, q:q + 1], SCALE, gains[:, q + 1:q + 2],
                                       ALU.mult, ALU.mult).then_inc(gqk_ready, 1)
            dve.wait_ge(vec_psum, 1)
            V.tensor_tensor(vec[:], ps_o[0:H_A, 0:VEC], vec_mask[:], ALU.add).then_inc(vec_ready, 1)
            dve.wait_ge(wf_hi_ready, 1)
            V.tensor_tensor(wf_lo[:], wf[:], wf_hi[:].bitcast(f32), ALU.subtract).then_inc(wf_ready, 1)

            def hidden_early(u, p, is_up):
                b, F = p + B_FFN_IN[u], p // 2 + u * FT
                add_halves(b)
                if is_up:
                    scaled(b, up[:], up_scaled)
                    wait(dve, up_scaled, F + 1)
                    wait(dve, silu_done, F + 1)
                    V.tensor_tensor(act_f[:], silu[:], up[:], ALU.mult).then_inc(act_done, 1)
                else:
                    wait(dve, rstd_ready, 2 * u + 1)
                    scaled(b, gate[:], gate_scaled)

            def hidden_late(u, p, is_up):
                if not is_up:
                    return
                F, f = p // 2 + u * FT, p // 2
                wait(dve, act_done, F + 1)
                wait(dve, act_hi, F + 1)
                hi = act[:, bass.ds(f.value(), 1), 0, :].rearrange("p a s -> p (a s)")
                lo = act[:, bass.ds(f.value(), 1), 1, :].rearrange("p a s -> p (a s)")
                V.tensor_tensor(lo, act_f[:], hi.bitcast(f32), ALU.subtract).then_inc(act_ready, 1)

            def add_to_x(b, j, factor, dest=None):
                wait(dve, block_summed, b + 1)
                V.scalar_tensor_tensor(x_tile(j) if dest is None else dest, total[:, b % 2, :], factor, x_tile(j),
                                       ALU.mult, ALU.add).then_inc(x_updated, 1)

            def out_early(u, j):
                b = j + B_FFN_OUT[u]
                add_halves(b)
                add_to_x(b, j, 0.5, x_final[:, j % 2, :] if u else None)

            def out_late(u, j):
                if u == 0:
                    x_split_lo(j + KT, j)

            def swiglu(u):
                if u:
                    x_mean_square(2)
                with dve.Fori(0, (2 * FT - 2) // UNROLL) as i:
                    for q in range(2, 2 + UNROLL):
                        n, p = Count(FFN_IN[u] + q, i, UNROLL), Count(q - 2, i, UNROLL)
                        split(n * 2)
                        hidden_early(u, p, q % 2)
                        split(n * 2 + 1)
                        hidden_late(u, p, q % 2)
                for q in range(UNROLL):
                    n = Count(FFN_OUT[u] + q)
                    split(n * 2, half_tiles(q % 3 * 2))
                    if q < 2:
                        hidden_early(u, Count(2 * FT - 2 + q), q)
                    if q == 4:
                        out_early(u, Count(0))
                    split(n * 2 + 1, half_tiles(q % 3 * 2 + 1))
                    if q < 2:
                        hidden_late(u, Count(2 * FT - 2 + q), q)
                    if q == 4:
                        out_late(u, Count(0))
                with dve.Fori(0, KT // 2 - 1) as i:
                    for q in range(UNROLL, 2 * UNROLL):
                        n = Count(FFN_OUT[u] + q, i, UNROLL)
                        j = Count((q - 4) // 3, i, 2)
                        split(n * 2, half_tiles(q % 3 * 2))
                        if q % 3 == 1:
                            out_early(u, j)
                        split(n * 2 + 1, half_tiles(q % 3 * 2 + 1))
                        if q % 3 == 1:
                            out_late(u, j)

            swiglu(0)

            def square(H, c, source):
                wait(dve, q_ready if c == 0 else k_ready, H + 1)
                V.tensor_tensor(hsq[:, c, :], source, source, ALU.mult).then_inc(squared, 1)

            def square_lo(H, c):
                wait(dve, squared_hi, H * 2 + (c + 1))
                V.tensor_tensor(hsq_lo[:, H % 2, c * SEQ:(c + 1) * SEQ], hsq[:, c, :],
                                hsq_hi[:, H % 2, c * SEQ:(c + 1) * SEQ].bitcast(f32), ALU.subtract).then_inc(squared_ready, 1)

            def head_mean_square(H):
                if H.exists():
                    wait(dve, hms_psum, H + 1)
                    V.tensor_scalar(hms[:], ps_st[:], EPS, -0.5, ALU.add, ALU.mult).then_inc(hms_ready, 1)

            def correct_head_rstd(H):
                if not H.exists():
                    return
                wait(dve, hrs_guessed, H + 1)
                V.tensor_tensor(hcorr[:], hrs[:], hrs[:], ALU.mult).then_inc(hcorr_step, 1)
                wait(dve, hcorr_step, H * 2 + 1)
                V.tensor_tensor(hcorr[:], hcorr[:], hms[:], ALU.mult).then_inc(hcorr_step, 1)
                wait(dve, hcorr_step, H * 2 + 2)
                V.scalar_tensor_tensor(hrs[:], hcorr[:], 1.5, hrs[:], ALU.add, ALU.mult).then_inc(hrs_ready, 1)

            def norm_qk(H):
                if H.exists():
                    wait(dve, hrs_ready, H + 1)
                    V.tensor_tensor(qn[:], qT[:, H % 2, :], hrs[:, 0:SEQ], ALU.mult).then_inc(qn_ready, 1)
                    V.scalar_tensor_tensor(kn[:], kT[:], gqk[:, H % 2:H % 2 + 1], hrs[:, SEQ:2 * SEQ],
                                           ALU.mult, ALU.mult).then_inc(kn_ready, 1)

            def softmax_max(H):
                if not H.exists():
                    return
                wait(dve, logit_psum, H + 1)
                V.tensor_tensor(prob[:], ps_l[:, 0:3 * P], d_tile(H, 0, 3 * P), ALU.add).then_inc(logit_ready, 1)
                wait(dve, logit_ready, H + 1)
                for b in range(TB):
                    last = V.reduce_max(mx[:, b:b + 1], prob[:, b * P:b * P + (b + 1) * P], AX.X)
                last.then_inc(max_ready, 1)
                wait(dve, max_ready, H + 1)
                V.tensor_scalar(nmx[:], mx[:], -1.0, None, ALU.mult).then_inc(nmax_ready, 1)

            def softmax_norm(H):
                if not H.exists():
                    return
                wait(dve, exp_ready, H + 1)
                if H % 2 == 0:
                    for b in range(TB):
                        c = slice(b * P, b * P + (b + 1) * P)
                        last = V.scalar_tensor_tensor(prob[:, c], prob[:, c], 1.0, mult[:, c], ALU.mult, ALU.mult,
                                                      accum_out=den[:, b:b + 1])
                    last.then_inc(den_ready, 1)
                    wait(dve, den_ready, H // 2 + 1)
                V.reciprocal(rden[:], den[:]).then_inc(rden_ready, 1)
                wait(dve, rden_ready, H + 1)
                for b in range(TB):
                    c = slice(b * P, b * P + (b + 1) * P)
                    last = V.tensor_scalar(pnorm[:, c], prob[:, c], rden[:, b:b + 1], None, ALU.mult)
                last.then_inc(prob_ready, 1)

            def mix_split_lo(H):
                if H.exists():
                    wait(dve, mix_hi, H + 1)
                    V.tensor_tensor(mix_tile(H, 1), ps_o[:, 0:SEQ], mix_tile(H, 0).bitcast(f32), ALU.subtract).then_inc(mix_ready, 1)

            def forget_gate():
                wait(dve, f_copied, 1)
                V.tensor_tensor(f_tot, f_main, ps_l[0:H_B, SEQ:2 * SEQ], ALU.add).then_inc(f_step, 1)
                wait(dve, f_step, 1)
                V.tensor_tensor(f_tot, f_tot, rstd[0:H_B, :], ALU.mult).then_inc(f_step, 1)
                wait(dve, f_step, 2)
                V.tensor_scalar(f_tot, f_tot, f_bias[:], None, ALU.add).then_inc(f_step, 1)
                wait(dve, f_step, 3)
                V.scalar_tensor_tensor(f_main, f_tot, -1.0, f_tot, ALU.mult, ALU.min).then_inc(f_step, 1)
                wait(dve, f_step, 4)
                V.tensor_scalar(f_tot, f_tot, -1.0, 0.0, ALU.mult, ALU.max).then_inc(f_step, 1)

            def forget_bias_tiles():
                wait(dve, ncum_psum, 1)
                V.tensor_copy(ncum[:], ps_st[:, 0:TB * H_B].rearrange("p (b h) -> p b h", b=TB)).then_inc(ncum_ready, 1)
                wait(dve, ncum_ready, 1)
                dve.wait_ge(mixer_loaded, 5 * 16)
                for h in range(H_B):
                    wait(dve, row_psum, h + 1)
                    for b in range(TB):
                        lo, hi = b * P, b * P + (b + 1) * P
                        last = V.scalar_tensor_tensor(d_tile(Count(2 * h + 1), lo, hi), row_banks[h % 2][:, 0:(b + 1) * P],
                                                      ncum[:, b, h:h + 1], causal[:, lo:hi], ALU.subtract, ALU.add)
                    last.then_inc(d_built, 1)
                wait(dve, d_built, H_B)

            def head_slots(H, forget=False):
                n, b = H * 3 + (HEADS + 2), H * 3 + B_HEADS
                split(n * 2)
                if forget:
                    x_mean_square(1)
                add_halves(b)
                if forget:
                    wait(dve, rstd_ready, 2)
                scaled(b, qT[:, H % 2, :], q_ready)
                square(H, 0, qT[:, H % 2, :])
                if forget:
                    forget_gate()
                correct_head_rstd(H - 1)
                norm_qk(H - 1)
                split(n * 2 + 1)
                if forget:
                    wait(dve, f_step, 5)
                    wait(dve, f_exped, 2)
                    V.tensor_tensor(f_tot, f_tot, f_exp, ALU.add).then_inc(nlf_ready, 1)
                square_lo(H, 0)

                split((n + 1) * 2)
                add_halves(b + 1)
                wait(dve, kn_ready, H)
                scaled(b + 1, kT[:], k_ready)
                square(H, 1, kT[:])
                split((n + 1) * 2 + 1)
                square_lo(H, 1)

                split((n + 2) * 2)
                add_halves(b + 2)
                scaled(b + 2, vT[:], v_ready)
                if forget:
                    forget_bias_tiles()
                softmax_max(H - 1)
                mix_split_lo(H - 2)
                split((n + 2) * 2 + 1)
                head_mean_square(H)
                softmax_norm(H - 1)

            split(Count(2 * HEADS))
            split(Count(2 * HEADS + 1))
            split(Count(2 * HEADS + 2))
            out_early(0, Count(KT - 1))
            split(Count(2 * HEADS + 3))
            out_late(0, Count(KT - 1))
            for H in range(4):
                head_slots(Count(H), H == 0)
            with dve.Fori(0, N_HEADS // 2 - 2) as i:
                for g in range(2):
                    head_slots(Count(4 + g, i, 2))
            last_head = N_HEADS - 1
            correct_head_rstd(Count(last_head))
            norm_qk(Count(last_head))
            mix_split_lo(Count(last_head - 1))
            softmax_max(Count(last_head))
            softmax_norm(Count(last_head))
            mix_split_lo(Count(last_head))

            def mixed_slot(n, j):
                b = j + B_W_OUT
                split(n * 2)
                add_halves(b)
                add_to_x(b, j, 1.0)
                split(n * 2 + 1)
                x_split_lo(j + 2 * KT, j)

            for j in range(2):
                mixed_slot(Count(W_OUT + 2 + j), Count(j))
            with dve.Fori(0, (KT - 4) // UNROLL) as i:
                for q in range(UNROLL):
                    mixed_slot(Count(W_OUT + 4 + q, i, UNROLL), Count(2 + q, i, UNROLL))
            for j in range(2):
                mixed_slot(Count(FFN_IN[1] + j), Count(KT - 2 + j))
            swiglu(1)
            out_early(1, Count(KT - 1))


def buckets():
    d = np.arange(SEQ, dtype=np.float32)
    exact = NUM_BUCKETS // 2
    large = exact + (np.log(np.maximum(d, np.float32(1)) / np.float32(exact)) / np.float32(math.log(MAX_DISTANCE / exact))
                     * np.float32(NUM_BUCKETS - exact)).astype(np.int32)
    return np.where(np.arange(SEQ) < exact, np.arange(SEQ), np.minimum(large, NUM_BUCKETS - 1))


def constants():
    dist = np.arange(SEQ)
    count = sum(((dist % d == 0) & (dist <= w)).astype(np.float32) for w, d in PATTERNS)
    one_hot = np.zeros((NUM_BUCKETS, VEC), np.float32)
    vec_mask = np.full((H_A, VEC), MASKED, np.float32)
    for d, bucket in enumerate(buckets()):
        if count[d]:
            one_hot[bucket, SEQ - 1 - d] = 1
            vec_mask[:, SEQ - 1 - d] = 0
    p = np.arange(P)[:, None]
    delta = np.concatenate([p - np.arange(P)[None], P + p - np.arange(SEQ)[None]], axis=1)
    c_mult = np.where(delta >= 0, count[np.maximum(delta, 0)], 0).astype(np.float32)
    c_causal = np.where(delta >= 0, 0, MASKED).astype(np.float32)
    j = np.arange(TB)[None, :, None] * P + np.arange(P)[:, None, None]
    c_upper = (j <= np.arange(SEQ)[None, None, :]).astype(np.float32)
    return {"c_one_hot": one_hot, "c_vec_mask": vec_mask, "c_mult": c_mult, "c_causal": c_causal, "c_upper": c_upper}


def kernel(**inputs):
    import concourse.bacc as bacc
    from concourse.bass_utils import run_bass_kernel_spmd

    nc = bacc.Bacc("TRN2", target_bir_lowering=False, num_devices=1)
    arrays = {name: np.ascontiguousarray(a) for name, a in {**inputs, **constants()}.items()}
    io = {name: nc.dram_tensor(name, a.shape, mybir.dt.from_np(a.dtype), kind="ExternalInput").ap() for name, a in arrays.items()}
    out = nc.dram_tensor("out", (1, SEQ, D_MODEL), mybir.dt.float32, kind="ExternalOutput").ap()
    layer(nc, io, out)
    result = run_bass_kernel_spmd(nc, [arrays], core_ids=[0])
    return result.results[0]["out"]
```
